# Optimizing a Trainium2 kernel written in Bass

```python
import jax, jax.numpy as jnp
from jax import lax
import numpy as np

D_MODEL = 2048
BATCH = 1
SEQ = 256
DEPTH = 2
DEC_BATCH = 8
DEC_SEQ = 8
PAST_LEN = 2048
PAGE_SIZE = 128

BRANCH = D_MODEL // 2
N_BRANCH = 3
A_HEADS = 16
A_KV_HEADS = 4
A_HEAD_DIM = BRANCH // A_HEADS
A_GROUP = A_HEADS // A_KV_HEADS
WINDOW = 128
ROPE_THETA = 10000.0
POOL_WINDOWS = (2, 4, 8, 16)
POOL_GROUPS = 4
POOL_GROUP_DIM = BRANCH // POOL_GROUPS
POOL_HIST = 15
C_HEADS = 4
C_KEY = BRANCH // 2
C_DK = C_KEY // C_HEADS
C_DV = BRANCH // C_HEADS
C_GATE_RANK = 16
C_GATE_TAU = 16.0
GLA_CHUNK = 64
EPS = 1e-6

SPLITS = (BRANCH, A_KV_HEADS * A_HEAD_DIM, A_KV_HEADS * A_HEAD_DIM, BRANCH,
          BRANCH, BRANCH,
          C_KEY, C_KEY, BRANCH, C_GATE_RANK, BRANCH,
          N_BRANCH * D_MODEL)
IN_COLS = sum(SPLITS)

kernel_name = 'hybrid_swa_pool_gla_gated_step'

def rms_norm(x, g):
    xf = x.astype(jnp.float32)
    y = xf * lax.rsqrt(jnp.mean(xf * xf, axis=-1, keepdims=True) + EPS)
    return (y * g.astype(jnp.float32)).astype(x.dtype)

def rope(x, pos):
    d = x.shape[-1]
    half = d // 2
    inv = jnp.power(ROPE_THETA, -jnp.arange(half, dtype=jnp.float32) * (2.0 / d))
    ang = pos.astype(jnp.float32)[:, None] * inv[None, :]
    cos = jnp.cos(ang)[None, :, None, :]
    sin = jnp.sin(ang)[None, :, None, :]
    xf = x.astype(jnp.float32)
    x1, x2 = xf[..., :half], xf[..., half:]
    return jnp.concatenate([x1 * cos - x2 * sin, x2 * cos + x1 * sin], axis=-1).astype(x.dtype)

def sink_attention(q, k, v, q_pos, k_pos, sinks):
    s = jnp.einsum('bnqhgd,bnkhd->bnhgqk', q, k, preferred_element_type=jnp.float32) * (A_HEAD_DIM ** -0.5)
    diff = q_pos[:, :, None] - k_pos[:, None, :]
    mask = (k_pos[:, None, :] >= 0) & (diff >= 0) & (diff <= WINDOW)
    s = jnp.where(mask[None, :, None, None], s, -jnp.inf)
    sink = sinks.astype(jnp.float32).reshape(1, 1, A_KV_HEADS, A_GROUP, 1, 1)
    m = jnp.maximum(jnp.max(s, axis=-1, keepdims=True), sink)
    p = jnp.exp(s - m)
    den = jnp.sum(p, axis=-1, keepdims=True) + jnp.exp(sink - m)
    p = (p / den).astype(v.dtype)
    return jnp.einsum('bnhgqk,bnkhd->bnqhgd', p, v)

def multiscale_pool(u, prev, start, w_pool, scale):
    bsz, L, _ = u.shape
    ext = jnp.concatenate([prev.astype(u.dtype), u], axis=1)
    cs = jnp.pad(jnp.cumsum(ext.astype(jnp.float32), axis=1), ((0, 0), (1, 0), (0, 0)))
    pos = start + jnp.arange(L)
    uf = u.astype(jnp.float32)
    hi = POOL_HIST + 1
    outs = []
    for g, w in enumerate(POOL_WINDOWS):
        sl = slice(g * POOL_GROUP_DIM, (g + 1) * POOL_GROUP_DIM)
        win_sum = cs[:, hi:hi + L, sl] - cs[:, hi - w:hi - w + L, sl]
        count = jnp.minimum(w, pos + 1).astype(jnp.float32)[None, :, None]
        outs.append(win_sum / count - uf[:, :, sl])
    d = jnp.stack(outs, axis=2).astype(u.dtype)
    y = jnp.einsum('blgc,gce->blge', d, w_pool).reshape(bsz, L, BRANCH)
    return y * scale, ext[:, -POOL_HIST:]

def gla_chunked(q, k, v, log_a, s0):
    bsz, L, H, _ = q.shape
    C = min(GLA_CHUNK, L)
    pad = (-L) % C
    nc = (L + pad) // C

    def prep(t):
        t = jnp.pad(t.astype(jnp.float32), ((0, 0), (0, pad), (0, 0), (0, 0)))
        return t.reshape(bsz, nc, C, H, t.shape[-1]).transpose(1, 0, 3, 2, 4)

    qc, kc, vc, ac = prep(q), prep(k), prep(v), prep(log_a)
    causal = jnp.tril(jnp.ones((C, C), dtype=bool))[:, :, None]

    def step(S, inp):
        qi, ki, vi, ai = inp
        b = jnp.cumsum(ai, axis=2)
        o = jnp.einsum('bhtd,bhde->bhte', qi * jnp.exp(b), S)
        decay = jnp.exp(jnp.where(causal, b[:, :, :, None, :] - b[:, :, None, :, :], -jnp.inf))
        att = jnp.einsum('bhtd,bhsd,bhtsd->bhts', qi, ki, decay)
        o = o + jnp.einsum('bhts,bhse->bhte', att, vi)
        b_last = b[:, :, -1:, :]
        S = jnp.exp(b_last[:, :, 0, :])[..., None] * S + jnp.einsum('bhsd,bhse->bhde', ki * jnp.exp(b_last - b), vi)
        return S, o

    S, o = lax.scan(step, s0.astype(jnp.float32), (qc, kc, vc, ac))
    o = o.transpose(1, 0, 3, 2, 4).reshape(bsz, L + pad, H, v.shape[-1])[:, :L]
    return o.astype(q.dtype), S

def trunk_layer(x, start, kv_buf, pool_prev, gla_state, norm_g, w_in, q_norm_g, k_norm_g, sinks,
                w_pool, pool_scale, w_gate_lr, b_gate, gla_norm_g, w_branch, w_out):
    bsz, L, _ = x.shape
    h = rms_norm(x, norm_g)
    proj = h @ w_in
    (a_q, a_k, a_v, a_z, b_u, b_z, c_q, c_k, c_v, c_lr, c_z, gates) = jnp.split(
        proj, np.cumsum(SPLITS)[:-1].tolist(), axis=-1)
    pos = start + jnp.arange(L)

    q = rope(rms_norm(a_q.reshape(bsz, L, A_HEADS, A_HEAD_DIM), q_norm_g), pos)
    k = rope(rms_norm(a_k.reshape(bsz, L, A_KV_HEADS, A_HEAD_DIM), k_norm_g), pos)
    v = a_v.reshape(bsz, L, A_KV_HEADS, A_HEAD_DIM)
    if kv_buf is None:
        nb = L // WINDOW
        qb = q.reshape(bsz, nb, WINDOW, A_KV_HEADS, A_GROUP, A_HEAD_DIM)

        def band(t):
            tp = jnp.pad(t, ((0, 0), (WINDOW, 0), (0, 0), (0, 0))).reshape(bsz, nb + 1, WINDOW, A_KV_HEADS, A_HEAD_DIM)
            return jnp.concatenate([tp[:, :-1], tp[:, 1:]], axis=2)

        kb, vb = band(k), band(v)
        q_pos = pos.reshape(nb, WINDOW)
        k_pos = (jnp.arange(nb)[:, None] - 1) * WINDOW + jnp.arange(2 * WINDOW)[None, :] + start
        new_k, new_v = k[:, -WINDOW:], v[:, -WINDOW:]
    else:
        ck, cv = kv_buf
        kk = jnp.concatenate([ck.astype(k.dtype), k], axis=1)
        vv = jnp.concatenate([cv.astype(v.dtype), v], axis=1)
        qb = q.reshape(bsz, 1, L, A_KV_HEADS, A_GROUP, A_HEAD_DIM)
        kb, vb = kk[:, None], vv[:, None]
        q_pos = pos[None]
        k_pos = jnp.concatenate([start - WINDOW + jnp.arange(WINDOW), pos])[None]
        new_k, new_v = kk[:, -WINDOW:], vv[:, -WINDOW:]
    o_a = sink_attention(qb, kb, vb, q_pos, k_pos, sinks).reshape(bsz, L, BRANCH)

    o_b, new_pool = multiscale_pool(b_u, pool_prev, start, w_pool, pool_scale)

    gq = c_q.reshape(bsz, L, C_HEADS, C_DK) * (C_DK ** -0.5)
    gk = c_k.reshape(bsz, L, C_HEADS, C_DK)
    gv = c_v.reshape(bsz, L, C_HEADS, C_DV)
    log_a = jax.nn.log_sigmoid((c_lr @ w_gate_lr + b_gate).astype(jnp.float32)) / C_GATE_TAU
    o_c, new_S = gla_chunked(gq, gk, gv, log_a.reshape(bsz, L, C_HEADS, C_DK), gla_state)
    o_c = rms_norm(o_c, gla_norm_g).reshape(bsz, L, BRANCH)

    branches = jnp.stack([o_a * jax.nn.silu(a_z), o_b * jax.nn.silu(b_z), o_c * jax.nn.silu(c_z)], axis=2)
    br = jnp.einsum('blnc,ncd->blnd', branches, w_branch)
    g = jax.nn.sigmoid(gates.reshape(bsz, L, N_BRANCH, D_MODEL).astype(jnp.float32))
    merged = jnp.sum(g * br.astype(jnp.float32), axis=2).astype(x.dtype)
    y = x + merged @ w_out
    return y, new_k, new_v, new_pool, new_S.astype(x.dtype)

def setup_inputs(seed: int = 0) -> dict:
    key = jax.random.key(seed)
    ks = jax.random.split(key, 20)
    f32 = jnp.float32
    nrm = lambda k, shape: jax.random.normal(k, shape, dtype=f32)
    return {
        'x_prompt': nrm(ks[0], (BATCH, SEQ, D_MODEL)),
        'x_sample': nrm(ks[1], (DEC_BATCH, DEC_SEQ, D_MODEL)),
        'cache_a_k': nrm(ks[2], (DEPTH, DEC_BATCH, WINDOW, A_KV_HEADS, A_HEAD_DIM)),
        'cache_a_v': nrm(ks[3], (DEPTH, DEC_BATCH, WINDOW, A_KV_HEADS, A_HEAD_DIM)),
        'state_pool': nrm(ks[4], (DEPTH, DEC_BATCH, POOL_HIST, BRANCH)),
        'state_gla': nrm(ks[5], (DEPTH, DEC_BATCH, C_HEADS, C_DK, C_DV)),
        'norm_g': 1.0 + 0.02 * nrm(ks[6], (DEPTH, D_MODEL)),
        'w_in': nrm(ks[7], (DEPTH, D_MODEL, IN_COLS)) * D_MODEL ** -0.5,
        'q_norm_g': 1.0 + 0.02 * nrm(ks[8], (DEPTH, A_HEAD_DIM)),
        'k_norm_g': 1.0 + 0.02 * nrm(ks[9], (DEPTH, A_HEAD_DIM)),
        'sinks': nrm(ks[10], (DEPTH, A_HEADS)),
        'w_pool': nrm(ks[11], (DEPTH, POOL_GROUPS, POOL_GROUP_DIM, POOL_GROUP_DIM)) * POOL_GROUP_DIM ** -0.5,
        'pool_scale': 1.0 + 0.02 * nrm(ks[12], (DEPTH, BRANCH)),
        'w_gate_lr': nrm(ks[13], (DEPTH, C_GATE_RANK, C_KEY)) * C_GATE_RANK ** -0.5,
        'b_gate': 0.1 * nrm(ks[14], (DEPTH, C_KEY)),
        'gla_norm_g': 1.0 + 0.02 * nrm(ks[15], (DEPTH, C_DV)),
        'w_branch': nrm(ks[16], (DEPTH, N_BRANCH, BRANCH, D_MODEL)) * BRANCH ** -0.5,
        'w_out': nrm(ks[17], (DEPTH, D_MODEL, D_MODEL)) * D_MODEL ** -0.5,
    }

def reference(x_prompt, x_sample, cache_a_k, cache_a_v, state_pool, state_gla, norm_g, w_in, q_norm_g,
              k_norm_g, sinks, w_pool, pool_scale, w_gate_lr, b_gate, gla_norm_g, w_branch, w_out):
    yp, ys = x_prompt, x_sample
    pool0 = jnp.zeros((x_prompt.shape[0], POOL_HIST, BRANCH), x_prompt.dtype)
    gla0 = jnp.zeros((x_prompt.shape[0], C_HEADS, C_DK, C_DV), jnp.float32)
    pk, pv, pp, ps, sk, sv, sp, ss = [], [], [], [], [], [], [], []
    for l in range(DEPTH):
        params = (norm_g[l], w_in[l], q_norm_g[l], k_norm_g[l], sinks[l], w_pool[l], pool_scale[l],
                  w_gate_lr[l], b_gate[l], gla_norm_g[l], w_branch[l], w_out[l])
        yp, a, b, c, d = trunk_layer(yp, 0, None, pool0, gla0, *params)
        pk.append(a); pv.append(b); pp.append(c); ps.append(d)
        ys, a, b, c, d = trunk_layer(ys, PAST_LEN, (cache_a_k[l], cache_a_v[l]), state_pool[l], state_gla[l], *params)
        sk.append(a); sv.append(b); sp.append(c); ss.append(d)
    return (yp, ys, jnp.stack(pk), jnp.stack(pv), jnp.stack(pp), jnp.stack(ps),
            jnp.stack(sk), jnp.stack(sv), jnp.stack(sp), jnp.stack(ss))


_drawn_inputs = setup_inputs


def setup_inputs(seed=0):
    import zlib

    import numpy as np

    out = dict(_drawn_inputs(seed))
    spreads = {}
    factors = {'q_norm_g': 58.575, 'sinks': 32.271, 'pool_scale': 7.561, 'gla_norm_g': 6.427}
    for name, (base, spread) in spreads.items():
        noise = np.random.default_rng([zlib.crc32(name.encode()), seed]).standard_normal(out[name].shape)
        drawn = base * np.exp(spread * noise) if base else spread * noise
        out[name] = __import__('jax').numpy.asarray(drawn.astype(out[name].dtype))
    for name, factor in factors.items():
        out[name] = (out[name] * factor).astype(out[name].dtype)
    return out
```

```python
from contextlib import ExitStack

import concourse.bass as bass
from concourse import mybir

F32 = mybir.dt.float32
F32R = mybir.dt.float32r
BF16 = mybir.dt.bfloat16
U8 = mybir.dt.uint8
ALU = mybir.AluOpType
ACT = mybir.ActivationFunctionType
AX = mybir.AxisListType

P = 128
DEPTH = 2
D = 2048
BRANCH = 1024
SEQ = 256
NB = 8
TS = 8
SMP = NB * TS
TOK = SEQ + SMP
KT_D = D // P
WINDOW = 128
HEADS = 16
KVH = 4
HD = 64
GH = 4
DK = 128
DV = 256
RANK = 16
HIST = 15
PAST = 2048
EPS = 1e-6
LEVELS = [1, 2, 4, 8, 16, 32, 64]

G_CQ, G_CK, G_CV, G_U, G_BZ, G_K, G_V, G_Q, G_CZ, G_AZ = 0, 2, 4, 8, 12, 16, 17, 18, 22, 26
N_IN = 30
LR_BEATS = 2
IN_BEATS = LR_BEATS + 4 * N_IN
PAIRS = D // 256
MIX_BEATS = PAIRS * 3 * 6
OUT_BEATS = PAIRS * 4
BEATS = IN_BEATS + MIX_BEATS + OUT_BEATS
GROUPS = 1 + N_IN + PAIRS * 6 + PAIRS
BR_A, BR_B, BR_C = 0, 1, 2

C_COS, C_SIN, C_IDENT, C_BLOCK, C_KEEP, C_INVC, C_BSEL, C_END = 0, 320, 640, 768, 896, 1216, 1280, 1288
R_NG, R_QG, R_KG, R_SINK, R_SSINK, R_PS, R_BG, R_GG, R_END = 0, 16, 17, 18, 34, 35, 43, 47, 49


def side_steps():
    at = {}

    def put(beat, name, k, banks):
        at.setdefault(beat, []).append((name, k, banks))

    put(2, "gate", 0, (0, 1, 2, 3))
    for k in range(8):
        put(19 + 2 * k, "level", k, (0, 1, 2) if k <= 3 else (0, 1))
    for k in range(4):
        put(22 + 4 * k, "v_turn_prompt", k, (3,))
        put(23 + 4 * k, "v_turn_sample", k, (3,))
    put(36, "k_turn", 0, (0, 1, 2))
    for k in range(4):
        put(39 + 4 * k, "pool", k, (2, 3))
    put(41, "first_chunk", 0, (0, 1, 2, 3))
    put(45, "second_chunk", 0, (0, 1, 2, 3))
    for k in range(8):
        put(52 + 2 * k, "sample_gla", k, (0, 1, 3))
    for k in range(2):
        put(68 + 2 * k, "gla_norm", k, (0, 1))
    put(71, "k_norm", 0, (2, 3))
    put(74, "kv_turn", 0, (2, 3))
    for k in range(4):
        put(79 + 4 * k, "q_norm", k, (2, 3))
    for j in range(8):
        n, banks = (80 + 4 * j, (0, 1)) if j < 3 else (92 + 2 * (j - 3), ((2, 3), (0, 1))[(j - 3) % 2])
        put(n, "scores", j, banks)
        put(n + 2, "p_turn", j, banks)
        put(n + 3, "pv", j, banks)
    for k in range(4):
        n = 102 + 2 * k
        put(n, "sample_scores", k, ((0,), (1,))[k % 2])
        put(n + 2, "sample_p_turn", k, ((0,), (1,))[k % 2])
        put(n + 3, "sample_pv", k, (2,))
    return at


STEPS = side_steps()
ORDER = [(n, k) for b in sorted(STEPS) for n, k, _ in STEPS[b]]
BANKS = {(n, k): banks for b in STEPS for n, k, banks in STEPS[b]}
STEP_NO = {s: i for i, s in enumerate(ORDER)}
N_STEPS = len(ORDER)
TAKE = {g: LR_BEATS + 4 * g + 3 for g in range(N_IN)}
TAKE.update({26: 112, 27: 115, 28: 118})
TAKEN_AT = {b: g for g, b in TAKE.items()}


def slot_banks(j):
    return BANKS[("scores", j)]


def trunk(nc, ins, outs):
    with ExitStack() as ctx:
        def sem(name):
            return ctx.enter_context(nc.semaphore(name))

        top = [nc.sbuf_base + 64 - nc.sbuf_base % 64]

        def place(name, shape, dt=F32, at=None):
            size = {F32: 4, F32R: 4, BF16: 2, U8: 1}[dt]
            for s in shape[1:]:
                size *= s
            if at is None:
                at = top[0]
                top[0] += -(-size // 64) * 64
            return nc.alloc_sbuf_tensor_at(name, shape, dt, offset=at)

        xg_hi = place("xg_hi", [P, KT_D, TOK], F32R)
        xg_lo = place("xg_lo", [P, KT_D, TOK], F32R)
        mix0 = top[0]
        mg_hi = place("mg_hi", [P, KT_D, TOK], F32R)
        mg_lo = place("mg_lo", [P, KT_D, TOK], F32R)
        br0 = top[0]
        T1 = TOK * 4
        part_b, part_c, part_a = br0, br0 + 16 * T1, br0 + 32 * T1
        top[0] += 48 * T1
        br_hi = [None] * 3
        br_lo = [None] * 3
        for n, at in ((BR_B, part_b), (BR_C, part_c), (BR_A, part_a)):
            br_hi[n] = place(f"branch_hi{n}", [P, 8, TOK], F32R, at=at)
            br_lo[n] = place(f"branch_lo{n}", [P, 8, TOK], F32R, at=at + 8 * T1)
        raw = [place(f"raw{i}", [P, 1024]) for i in range(4)]
        w_hi = [place(f"w_hi{i}", [P, 512], F32R) for i in range(4)]
        w_lo = [place(f"w_lo{i}", [P, 512], F32R) for i in range(4)]
        const = place("const", [P, C_END])
        amask_p = place("amask_p", [P, 256], BF16)
        amask_s = place("amask_s", [P, 128 + NB * SMP], BF16)
        gmask = place("gmask", [P, 8, P], U8)
        par = place("par", [P, DEPTH, R_END])
        ones = place("ones", [P, P])
        eps = place("eps", [P, 1])
        rstd = place("rstd", [P, TOK])
        ta0 = top[0]
        ta = place("ta", [P, 2, TOK])
        tb = place("tb", [P, 2, TOK])
        tc = place("tc", [P, 2, TOK])
        att_s = place("att_s", [P, GH * SMP])
        small = place("small", [P, 64])
        edge = place("edge", [P, GH, 2 + NB])
        q_s = place("q_s", [P, 2, NB, 2, 4, TS])
        att0 = top[0]
        att_p = place("att_p", [P, 2, 512])
        probs0 = place("probs0", [P, 768])
        probs1 = place("probs1", [P, 768], at=att0)
        sq_sum = place("sq_sum", [P, TOK], at=att0)
        x_first = place("x_first", [P, KT_D, TOK], at=mix0)
        gmask_f = place("gmask_f", [P, 8, P], at=mix0 + 16 * T1)
        o_c = place("o_c", [P, 8, TOK], at=mix0)
        o_ab = place("o_ab", [P, 8, TOK], at=mix0 + 8 * T1)
        q_a = place("q_a", [P, 8, TOK], at=mix0 + 16 * T1)
        hist = place("hist", [P, 8, (1 + NB) * HIST], at=mix0 + 16 * T1)
        lev_e = place("lev_e", [P, GH, TOK], at=mix0 + 24 * T1)
        lev_k = place("lev_k", [P, GH, TOK], at=mix0 + 28 * T1)
        s1 = place("s1", [P, GH, DV], at=mix0 + 24 * T1)
        k_a = place("k_a", [P, 2, TOK], at=mix0 + 28 * T1)
        v_tok = place("v_tok", [P, 3, KVH * HD], at=mix0 + 24 * T1)
        EXT = HIST + SEQ + NB * (HIST + TS)
        ext = place("ext", [P, 2, EXT], at=part_b)
        sums = place("sums", [P, 2, EXT], at=part_b + 3648)
        sums2 = place("sums2", [P, 2, EXT], at=ta0)
        diff = place("diff", [P, 2, TOK], at=part_b + 7296)
        w_pool = place("w_pool", [P, 8, 256], at=part_b + 7296 + 2560)
        v_gla = place("v_gla", [P, 3, 1024], at=part_c)
        ko_tok = place("ko_tok", [P, 3, GH * DK], at=part_c + 12288)
        k_sel = place("k_sel", [P, 4, DK], at=part_c + 12288 + 6144)
        squares = place("squares", [P, 4, TOK], at=part_c)
        w_gate = place("w_gate", [P, GH * DK], at=part_c + 12288 + 6144)
        cq = place("cq", [P, GH, TOK], at=part_a)
        ck = place("ck", [P, GH, TOK], at=part_a + 4 * T1)
        cb = place("cb", [P, GH, TOK], at=part_a + 8 * T1)
        lev_q = place("lev_q", [P, GH, TOK], at=part_a + 12 * T1)
        state = place("state", [P, 2, 4, DV], at=part_a)
        cache_k = place("cache_k", [P, 2, NB, WINDOW], at=part_a)
        cache_v = place("cache_v", [P, NB, KVH * HD], at=part_a + 8192)
        probs = [probs0, probs1]

        main = ctx.enter_context(nc.psum_tensor("main", [P, 4, 512], F32))
        side = ctx.enter_context(nc.psum_tensor("side", [P, 4, 512], F32))
        rms_psum = side[:, 0, 0:TOK]

        raw_in = [sem(f"raw_in{i}") for i in range(4)]
        hi_ready = sem("hi_ready")
        lo_ready = sem("lo_ready")
        half_used = sem("half_used")
        main_free = sem("main_free")
        step_done = sem("step_done")
        vec_done = sem("vec_done")
        act_done = sem("act_done")
        act_given = sem("act_given")
        rms_done = sem("rms_done")
        consts_in = sem("consts_in")
        x_in = [sem(f"x_in{j}") for j in range(8)]
        hist_in = sem("hist_in")
        w_pool_in = sem("w_pool_in")
        w_gate_in = sem("w_gate_in")
        state_in = [sem(f"state_in{i}") for i in range(2)]
        caches_in = sem("caches_in")
        res_in = [sem(f"res_in{i}") for i in range(2)]
        y_out = [sem(f"y_out{i}") for i in range(2)]
        state_out = [sem(f"state_out{i}") for i in range(2)]
        hist_out = sem("hist_out")
        kv_out = sem("kv_out")
        s2_out = sem("s2_out")
        window_out = sem("window_out")

        marks = {}

        def wait_mark(e, *key):
            s, v = marks[key]
            e.wait_ge(s, v)

        class Counted:

            def __init__(self, e, s):
                self.e, self.s, self.n, self.loop = e, s, 0, 0

            def value(self):
                return self.loop + self.n

            def __call__(self, instruction):
                instruction.then_inc(self.s, 1)
                self.n += 1

            def settle(self):
                self.e.wait_ge(self.s, self.value())

            def mark(self, *key):
                marks[key] = (self.s, self.value())

        def col(l, c, lo=0, hi=P):
            return par[lo:hi, l, c:c + 1]

        def two(t):
            return t.unsqueeze(1).to_broadcast([t.shape[0], 2, t.shape[1]])

        cosb = two(const[:, C_COS:C_COS + TOK])
        sinb = two(const[:, C_SIN:C_SIN + TOK])
        ident = const[:, C_IDENT:C_IDENT + P]
        head_ones = const[:, C_BLOCK:C_BLOCK + P]
        keep = const[:, C_KEEP:C_KEEP + TOK]

        def group_psum(G, n=2):
            b = 2 * (G % 2)
            return main[:, b:b + n, 0:TOK]

        def last_half(l, beat):
            return 2 * (BEATS * l + beat + 1)

        def segs(t3, B):
            n = TOK if B <= 4 else SEQ
            return t3[:, :, 0:n].rearrange("p h (a b) -> p h a b", b=2 * B), n // (2 * B)

        block = ctx.enter_context(nc.Block())

        @block.vector
        def _(dve):
            v = Counted(dve, vec_done)
            given = [0]

            def from_act():
                given[0] += 1
                dve.wait_ge(act_given, loop_given[0] + given[0])

            loop_given = [0]
            free = [0]

            def split_lo(Q, s0):
                for s in range(2):
                    i = (2 * s0 + s) % 4
                    dve.wait_ge(hi_ready, Q * 2 + (s + 1))
                    dve.tensor_tensor(w_lo[i][:, :], raw[s0 % 4][:, 512 * s:512 * s + 512],
                                      w_hi[i][:, :].bitcast(F32), ALU.subtract).then_inc(lo_ready, 1)

            def wait_step(l, name, k):
                dve.wait_ge(step_done, N_STEPS * l + STEP_NO[(name, k)] + 1)

            def read_group(l, G, beat_end, op):
                dve.wait_ge(half_used, beat_end)
                op(group_psum(G)).then_inc(main_free, 1)

            def settle_group(G):
                dve.wait_ge(main_free, G + 1)

            def tt(out, a, b, op):
                v(dve.tensor_tensor(out, a, b, op))
                v.settle()

            def stt(out, a, s, b, op0, op1):
                v(dve.scalar_tensor_tensor(out, a, s, b, op0, op1))
                v.settle()

            v(dve.memset(ones[:, :], 1.0))
            v(dve.memset(eps[:, :], EPS))
            v(dve.memset(q_s[:, :, :, :, :, :].rearrange("p i b j g t -> p (i b j g t)"), 0.0))
            v.settle()
            v.mark("start", 0, 0)
            dve.wait_ge(consts_in, 80)
            v(dve.tensor_copy(gmask[:, :, :], gmask_f[:, :, :]))
            for j in range(8):
                from_act()
                for t in range(2):
                    c = 2 * j + t
                    v(dve.scalar_tensor_tensor(xg_lo[:, c, :], x_first[:, c, :], col(0, R_NG + c),
                                               xg_hi[:, c, :].bitcast(F32), ALU.mult, ALU.subtract))
                    if c == 0:
                        v(dve.tensor_tensor(sq_sum[:, :], x_first[:, c, :], x_first[:, c, :], ALU.mult))
                    else:
                        v(dve.tensor_tensor(tb[:, t, :], x_first[:, c, :], x_first[:, c, :], ALU.mult))
                        v.settle()
                        v(dve.tensor_tensor(sq_sum[:, :], sq_sum[:, :], tb[:, t, :], ALU.add))
                v.mark("xg", 0, j)
            v.settle()
            v.mark("sq_sum", 0, 0)

            def take(l, g):
                G = GROUPS * l + 1 + g
                end = last_half(l, LR_BEATS + 4 * g + 3)
                r2 = two(rstd[:, :])
                if g < G_CK:
                    read_group(l, G, end, lambda ps: dve.scalar_tensor_tensor(
                        cq[:, 2 * g:2 * g + 2, :], ps, float(DK) ** -0.5, r2, ALU.mult, ALU.mult))
                elif g < G_CV:
                    i = 2 * (g - G_CK)
                    read_group(l, G, end, lambda ps: dve.tensor_tensor(ck[:, i:i + 2, :], ps, r2, ALU.mult))
                elif g < G_U:
                    i = 2 * (g - G_CV)
                    read_group(l, G, end, lambda ps: dve.tensor_tensor(o_c[:, i:i + 2, :], ps, r2, ALU.mult))
                elif g < G_BZ:
                    pool_pair(l, g - G_U, G, end)
                elif g in (G_K, G_V) or G_Q <= g < G_CZ:
                    dst = ta if g != G_V else tb
                    if g == G_Q:
                        dve.wait_ge(kv_out, 48 * l + 48)
                    read_group(l, G, end, lambda ps: dve.tensor_tensor(dst[:, :, :], ps, r2, ALU.mult))
                else:
                    gate_pair(l, g, G, end)
                marks[("taken", l, g)] = (main_free, G + 1)
                if g < G_U or G_K <= g < G_CZ:
                    settle_group(G)

            def pool_pair(l, gi, G, end):
                w = 2 << gi
                dve.wait_ge(half_used, end)
                from_act()
                if gi:
                    wait_step(l, "pool", gi - 1)
                ps = group_psum(G)
                for t in range(2):
                    x = ext[:, t, :]
                    v(dve.tensor_tensor(x[:, HIST:HIST + SEQ], ps[:, t, 0:SEQ], rstd[:, 0:SEQ], ALU.mult))
                    out = x[:, HIST + SEQ:EXT].rearrange("p (b t) -> p b t", t=HIST + TS)[:, :, HIST:]
                    last = dve.tensor_tensor(out, ps[:, t, SEQ:TOK].rearrange("p (b t) -> p b t", t=TS),
                                             rstd[:, SEQ:TOK].rearrange("p (b t) -> p b t", t=TS), ALU.mult)
                    if t == 0:
                        v(last)
                last.then_inc(main_free, 1)
                settle_group(G)
                marks[("ext_full", l, gi)] = (main_free, G + 1)
                src, step = ext, 1
                for i in range(gi + 1):
                    n = 2 * step - 1
                    dst = (sums, sums2)[i % 2]
                    tt(dst[:, :, n:EXT], src[:, :, n:EXT], src[:, :, n - step:EXT - step], ALU.add)
                    src, step = dst, 2 * step
                stt(diff[:, :, 0:SEQ], src[:, :, HIST:HIST + SEQ], 1.0 / w, ext[:, :, HIST:HIST + SEQ],
                    ALU.mult, ALU.subtract)
                inv = two(const[:, C_INVC + 16 * gi:C_INVC + 16 * gi + 16])
                tt(tc[:, :, 0:16], src[:, :, HIST:HIST + 16], inv, ALU.mult)
                tt(diff[:, :, 0:16], tc[:, :, 0:16], ext[:, :, HIST:HIST + 16], ALU.subtract)
                for t in range(2):
                    def smp(z):
                        return z[:, t, HIST + SEQ:EXT].rearrange("p (b t) -> p b t", t=HIST + TS)[:, :, HIST:]
                    v(dve.scalar_tensor_tensor(diff[:, t, SEQ:TOK].rearrange("p (b t) -> p b t", t=TS), smp(src),
                                               1.0 / w, smp(ext), ALU.mult, ALU.subtract))
                v.settle()
                v.mark("diff", l, gi)

            def gate_pair(l, g, G, end):
                n, g0, o = ((BR_B, G_BZ, o_ab) if g < G_K else (BR_C, G_CZ, o_c) if g < G_AZ else (BR_A, G_AZ, o_ab))
                i = 2 * (g - g0)
                if g == G_BZ:
                    dve.wait_ge(hist_out, 16 * l + 16)
                read_group(l, G, end, lambda ps: dve.tensor_tensor(ta[:, :, :], ps, two(rstd[:, :]), ALU.mult))
                settle_group(G)
                marks[("z", l, g)] = (main_free, G + 1)
                from_act()
                tt(ta[:, :, :], ta[:, :, :], tc[:, :, :], ALU.mult)
                tt(ta[:, :, :], ta[:, :, :], o[:, i:i + 2, :], ALU.mult)
                v.mark("gated", l, g)
                from_act()
                v(dve.tensor_tensor(br_lo[n][:, i:i + 2, :], ta[:, :, :], br_hi[n][:, i:i + 2, :].bitcast(F32),
                                    ALU.subtract))
                v.mark("branch", l, g)

            def log_decay(l):
                wait_step(l, "gate", 0)
                for h in range(GH):
                    v(dve.tensor_scalar(cq[:, h, :], side[:, h, 0:TOK], col(l, R_BG + h), None, ALU.add))
                v.settle()
                v.mark("gate_in", l, 0)
                from_act()
                v(dve.tensor_scalar(ck[:, :, :], cq[:, :, :], 0.0, 1.0 / 16.0, ALU.min, ALU.mult))
                v.settle()
                stt(ck[:, :, :], lev_e[:, :, :], -1.0 / 16.0, ck[:, :, :], ALU.mult, ALU.add)
                for h in range(GH):
                    v(dve.tensor_tensor_scan(cb[:, h, :], keep, ck[:, h, :], 0.0, ALU.mult, ALU.add))
                v(dve.memset(att_p[:, :, :], 0.0))
                v(dve.memset(att_s[:, :], 0.0))
                v.settle()
                v.mark("decay", l, 0)

            def level_prep(l, k):
                B = LEVELS[k - 1]
                e4, n = segs(lev_e, B)
                b4, _ = segs(cb, B)
                if k > 1:
                    wait_step(l, "level", k - 1)
                for h in range(GH):
                    v(dve.tensor_tensor(e4[:, h], b4[:, h],
                                        b4[:, h, :, B - 1:B].to_broadcast([P, n, 2 * B]), ALU.subtract))
                v.mark("level_gap", l, k)
                from_act()
                w = n * 2 * B
                v(dve.tensor_tensor(lev_q[:, :, 0:w], cq[:, :, 0:w], lev_e[:, :, 0:w], ALU.mult))
                v(dve.tensor_tensor(lev_k[:, :, 0:w], ck[:, :, 0:w], lev_e[:, :, 0:w], ALU.mult))
                v.mark("level", l, k)

            def level_take(l, k):
                wait_step(l, "level", k)
                for c in range(2):
                    v(dve.copy_predicated(att_p[:, c, :].rearrange("p (h t) -> p h t", h=GH),
                                          gmask[:, k, :].unsqueeze(1).to_broadcast([P, GH, P]),
                                          side[:, c, :].rearrange("p (h t) -> p h t", h=GH)))
                if k <= 3:
                    v(dve.copy_predicated(att_s[0:SMP, :].rearrange("p (h t) -> p h t", h=GH),
                                          gmask[0:SMP, k, 0:SMP].unsqueeze(1).to_broadcast([SMP, GH, SMP]),
                                          side[0:SMP, 2, 0:GH * SMP].rearrange("p (h t) -> p h t", h=GH)))
                v.settle()
                v.mark("att", l, k)

            def carry_prep(l):
                wait_step(l, "level", 7)
                from_act()
                tt(lev_q[:, :, :], cq[:, :, :], lev_e[:, :, :], ALU.mult)
                for h in range(GH):
                    for lo, hi, n in ((0, SEQ, P), (SEQ, TOK, TS)):
                        b3 = cb[:, h, lo:hi].rearrange("p (a b) -> p a b", b=n)
                        v(dve.tensor_tensor(lev_e[:, h, lo:hi].rearrange("p (a b) -> p a b", b=n),
                                            b3[:, :, n - 1:n].to_broadcast([P, (hi - lo) // n, n]), b3, ALU.subtract))
                v.settle()
                v.mark("end_gap", l, 0)
                from_act()
                v(dve.tensor_tensor(lev_k[:, :, :], ck[:, :, :], lev_e[:, :, :], ALU.mult))
                v.settle()
                v.mark("carry", l, 0)

            def second_state(l):
                wait_step(l, "second_chunk", 0)
                for h in range(GH):
                    v(dve.scalar_tensor_tensor(s1[:, h, :], s1[:, h, :], edge[:, h, 1:2],
                                               side[:, 2 + h // 2, 256 * (h % 2):256 * (h % 2) + 256],
                                               ALU.mult, ALU.add))
                v.settle()
                v.mark("second_state", l, 0)

            def sample_sel(l, k):
                h, half = divmod(k, 2)
                if k:
                    wait_step(l, "sample_gla", k - 1)
                src = ko_tok[0:SMP, 2, DK * h:DK * h + DK].unsqueeze(1).to_broadcast([SMP, 4, DK])
                sel = const[0:SMP, C_BSEL + 4 * half:C_BSEL + 4 * half + 4].unsqueeze(2).to_broadcast([SMP, 4, DK])
                v(dve.tensor_tensor(k_sel[0:SMP, :, :], src, sel, ALU.mult))
                v.mark("k_sel", l, k)

            def sample_state(l, k):
                h, half = divmod(k, 2)
                wait_step(l, "sample_gla", k)
                for b in range(4):
                    v(dve.scalar_tensor_tensor(state[:, k % 2, b, :], state[:, k % 2, b, :],
                                               edge[:, h, 2 + 4 * half + b:3 + 4 * half + b],
                                               side[:, b // 2, 256 * (b % 2):256 * (b % 2) + 256],
                                               ALU.mult, ALU.add))
                v.settle()
                v.mark("sample_state", l, k)

            def gla_scale(l, k):
                from_act()
                v(dve.reciprocal(tb[:, :, :], tb[:, :, :]))
                v.settle()
                for i in range(2):
                    for t in range(2):
                        c = 4 * k + 2 * i + t
                        v(dve.scalar_tensor_tensor(o_c[:, c, :], o_c[:, c, :], col(l, R_GG + t), tb[:, i, :],
                                                   ALU.mult, ALU.mult))
                v.settle()
                v.mark("gla_scaled", l, k)

            def rope_pair(l, name, k):
                out, g = (k_a[:, :, :], R_KG) if name == "k_norm" else (q_a[:, 2 * k:2 * k + 2, :], R_QG)
                from_act()
                v(dve.reciprocal(tb[:, :, :], tb[:, :, :]))
                v.settle()
                stt(ta[:, :, :], ta[:, :, :], col(l, g), tb[:, :, :], ALU.mult, ALU.mult)
                v.mark("normed", l, (name, k))
                tt(out, ta[:, :, :], cosb, ALU.mult)
                from_act()
                tt(tc[:, :, :], tc[:, :, :], sinb, ALU.mult)
                tt(out, out, tc[:, :, :], ALU.add)
                if name == "q_norm":
                    for t in range(2):
                        for i in range(2):
                            rows = slice(HD * i, HD * i + HD)
                            v(dve.tensor_copy(q_s[rows, k // 2, :, i, 2 * (k % 2) + t, :],
                                              q_a[rows, 2 * k + t, SEQ:TOK].rearrange("p (b t) -> p b t", t=TS)))
                    v.settle()
                v.mark("roped", l, (name, k))

            def prompt_softmax(l, j):
                p = probs[j % 2]
                b0, b1 = slot_banks(j)
                wait_step(l, "scores", j)
                p2 = p[:, :].rearrange("p (h k) -> p h k", h=2)
                late = p2[:, :, 0:256]
                early = p2[:, :, 256:384]
                v(dve.scalar_tensor_tensor(late, side[:, b0:b0 + 2, 0:256], HD ** -0.5, two(amask_p[:, :]),
                                           ALU.mult, ALU.add))
                v(dve.scalar_tensor_tensor(early, side[:, b0:b0 + 2, 256:384], HD ** -0.5, two(amask_p[:, 128:256]),
                                           ALU.mult, ALU.add))
                v.settle()
                v(dve.tensor_reduce(small[:, 0:2], late, AX.X, ALU.max))
                v(dve.tensor_reduce(small[:, 2:4], early, AX.X, ALU.max))
                v.settle()
                sink = par[:, l, R_SINK + 2 * j:R_SINK + 2 * j + 2]
                for i in (0, 2):
                    v(dve.tensor_tensor(small[:, i:i + 2], small[:, i:i + 2], sink, ALU.max))
                v.settle()
                v(dve.tensor_scalar(small[:, 4:8], small[:, 0:4], -1.0, None, ALU.mult))
                for i in (0, 2):
                    v(dve.tensor_tensor(small[:, 8 + i:10 + i], sink, small[:, i:i + 2], ALU.subtract))
                v.settle()
                v.mark("masked", l, j)
                from_act()
                tt(small[:, 16:20], small[:, 12:16], small[:, 20:24], ALU.add)
                v(dve.reciprocal(small[:, 16:20], small[:, 16:20]))
                v.settle()
                for i in range(2):
                    v(dve.tensor_scalar(late[:, i], late[:, i], small[:, 16 + i:17 + i], None, ALU.mult))
                    v(dve.tensor_scalar(early[:, i], early[:, i], small[:, 18 + i:19 + i], None, ALU.mult))
                v.settle()
                v.mark("probs", l, j)

            def sample_softmax(l, k):
                p = probs[k % 2]
                b0, = BANKS[("sample_scores", k)]
                wait_step(l, "sample_scores", k)
                s3 = side[:, b0, 0:384].rearrange("p (b k) -> p b k", b=2)
                p3 = p[:, 0:384].rearrange("p (b k) -> p b k", b=2)
                new = amask_s[:, 128 + 2 * k * SMP:128 + 2 * (k + 1) * SMP].rearrange("p (b k) -> p b k", b=2)
                v(dve.scalar_tensor_tensor(p3[:, :, 0:128], s3[:, :, 0:128], HD ** -0.5, two(amask_s[:, 0:128]),
                                           ALU.mult, ALU.add))
                v(dve.scalar_tensor_tensor(p3[:, :, 128:192], s3[:, :, 128:192], HD ** -0.5, new, ALU.mult, ALU.add))
                v.settle()
                v(dve.tensor_reduce(small[:, 0:2], p3, AX.X, ALU.max))
                v.settle()
                v(dve.tensor_scalar(small[:, 0:2], small[:, 0:2], col(l, R_SSINK), None, ALU.max))
                v.settle()
                v(dve.tensor_scalar(small[:, 4:6], small[:, 0:2], -1.0, None, ALU.mult))
                v.settle()
                v(dve.tensor_scalar(small[:, 8:10], small[:, 4:6], col(l, R_SSINK), None, ALU.add))
                v.settle()
                v.mark("sample_masked", l, k)
                from_act()
                tt(small[:, 16:18], small[:, 12:14], small[:, 20:22], ALU.add)
                v(dve.reciprocal(small[:, 16:18], small[:, 16:18]))
                v.settle()
                for i in range(2):
                    v(dve.tensor_scalar(p3[:, i], p3[:, i], small[:, 16 + i:17 + i], None, ALU.mult))
                v.settle()
                v.mark("sample_probs", l, k)

            def vector_part(l, beat):
                if beat == 0:
                    from_act()
                    v(dve.reciprocal(rstd[:, :], rstd[:, :]))
                    v.settle()
                if beat == 1:
                    for i in range(2 if l else 0):
                        dve.wait_ge(y_out[i], 64 * l)
                    dve.wait_ge(half_used, last_half(l, 1))
                    dve.tensor_tensor(ta[:, 0, :], group_psum(GROUPS * l)[:, 0, :], rstd[:, :],
                                      ALU.mult).then_inc(main_free, 1)
                    marks[("lr", l, 0)] = (main_free, GROUPS * l + 1)
                if beat in TAKEN_AT:
                    take(l, TAKEN_AT[beat])
                for name, k, _ in STEPS.get(beat, ()):
                    if name == "gate":
                        log_decay(l)
                    elif name == "level":
                        level_take(l, k)
                    elif name == "pool":
                        wait_step(l, "pool", k)
                        for t in range(2):
                            v(dve.tensor_scalar(o_ab[:, 2 * k + t, :], side[:, 2 + t, 0:TOK],
                                                col(l, R_PS + 2 * k + t), None, ALU.mult))
                        v.settle()
                        v.mark("pooled", l, k)
                    elif name == "second_chunk":
                        second_state(l)
                    elif name == "sample_gla":
                        sample_state(l, k)
                    elif name == "gla_norm":
                        gla_scale(l, k)
                    elif name in ("k_norm", "q_norm"):
                        rope_pair(l, name, k)
                    elif name == "scores":
                        prompt_softmax(l, k)
                    elif name == "sample_scores":
                        sample_softmax(l, k)
                for k in range(1, 8):
                    if beat == 17 + 2 * k:
                        level_prep(l, k)
                if beat == 34:
                    carry_prep(l)
                for k in range(8):
                    if beat == 50 + 2 * k:
                        sample_sel(l, k)

            def mix_body(l, i, py):
                Q0 = BEATS * l + IN_BEATS
                G0 = GROUPS * l + 1 + N_IN
                b = 0
                for jj in range(2):
                    for n in range(3):
                        for part in range(6):
                            split_lo(i * 36 + (Q0 + b + 2), Q0 + b + 2)
                            b += 1
                            if part == 3:
                                dve.wait_ge(half_used, i * 72 + 2 * (Q0 + b))
                                dve.tensor_tensor(ta[:, :, :], group_psum(G0), two(rstd[:, :]),
                                                  ALU.mult).then_inc(main_free, 1)
                        dve.wait_ge(half_used, i * 72 + 2 * (Q0 + b))
                        from_act()
                        dst = tc if n == 0 else ta
                        v.settle()
                        dve.tensor_tensor(dst[:, :, :], group_psum(G0 + 1), tb[:, :, :],
                                          ALU.mult).then_inc(main_free, 1)
                        dve.wait_ge(main_free, i * 12 + (G0 + 6 * jj + 2 * n + 2))
                        if n:
                            tt(tc[:, :, :], tc[:, :, :], ta[:, :, :], ALU.add)
                    at = i * 4 + 2 * jj
                    hi = mg_hi[:, bass.ds(at, 2), :] if not py else mg_hi[:, at:at + 2, :]
                    lo = mg_lo[:, bass.ds(at, 2), :] if not py else mg_lo[:, at:at + 2, :]
                    v(dve.tensor_scalar(hi, tc[:, :, :], 1.0, None, ALU.mult))
                    v.settle()
                    v(dve.tensor_tensor(lo, tc[:, :, :], hi.bitcast(F32), ALU.subtract))

            def out_body(l, i, py, last_layer):
                Q0 = BEATS * l + IN_BEATS + MIX_BEATS
                G0 = GROUPS * l + 1 + N_IN + 6 * PAIRS
                for jj in range(2):
                    for part in range(4):
                        b = 4 * jj + part
                        if not (last_layer and py and b >= 6):
                            split_lo(i * 8 + (Q0 + b + 2), Q0 + b + 2)
                    y = (ta, tb)[jj]
                    dve.wait_ge(res_in[jj], i * 16 + (64 * l + 16))
                    dve.wait_ge(half_used, i * 16 + 2 * (Q0 + 4 * jj + 4))
                    dve.tensor_tensor(y[:, :, :], y[:, :, :], group_psum(G0 + jj), ALU.add).then_inc(main_free, 1)
                    dve.wait_ge(main_free, i * 2 + (G0 + jj + 1))
                    if not last_layer:
                        for t in range(2):
                            at = i * 4 + (2 * jj + t)
                            g = par[:, l + 1, R_NG:R_NG + KT_D][:, bass.ds(at, 1)]
                            hi = xg_hi[:, bass.ds(at, 1), :].rearrange("p a t -> p (a t)")
                            lo = xg_lo[:, bass.ds(at, 1), :].rearrange("p a t -> p (a t)")
                            v(dve.tensor_scalar(hi, y[:, t, :], g, None, ALU.mult))
                            v.settle()
                            v(dve.scalar_tensor_tensor(lo, y[:, t, :], g, hi.bitcast(F32), ALU.mult, ALU.subtract))
                            v(dve.tensor_tensor(tc[:, t, :], y[:, t, :], y[:, t, :], ALU.mult))
                            v.settle()
                            v(dve.tensor_tensor(sq_sum[:, :], sq_sum[:, :], tc[:, t, :], ALU.add))

            for l in range(DEPTH):
                last_layer = l == DEPTH - 1
                for beat in range(IN_BEATS):
                    Q = BEATS * l + beat
                    if l == 0 and beat == 0:
                        split_lo(0, 0)
                        split_lo(1, 1)
                    split_lo(Q + 2, Q + 2)
                    vector_part(l, beat)
                v.mark("branches", l, 0)
                v.settle()
                base_v, base_g = v.n, given[0]
                per_v, per_g = 2 * (2 + 2), 6
                with dve.Fori(0, 4) as i:
                    v.loop, loop_given[0] = i * per_v, i * per_g
                    mix_body(l, i, False)
                assert v.n - base_v == per_v and given[0] - base_g == per_g, (v.n - base_v, given[0] - base_g)
                v.loop, loop_given[0] = 0, 0
                v.n, given[0] = base_v + 4 * per_v, base_g + 4 * per_g
                v.settle()
                v.mark("merged", l, 0)
                if not last_layer:
                    v(dve.memset(sq_sum[:, :], 0.0))
                    v.settle()
                    base_v = v.n
                    per_v = 16
                    with dve.Fori(0, 4) as i:
                        v.loop = i * per_v
                        out_body(l, i, False, False)
                    assert v.n - base_v == per_v
                    v.loop, v.n = 0, base_v + 4 * per_v
                    for j in range(8):
                        marks[("xg", l + 1, j)] = (vec_done, base_v + 8 * j + 8)
                    v.settle()
                    v.mark("sq_sum", l + 1, 0)
                else:
                    with dve.Fori(0, 3) as i:
                        out_body(l, i, False, True)
                    out_body(l, 3, True, True)

        @block.scalar
        def _(act):
            a = Counted(act, act_done)

            def give(instruction):
                instruction.then_inc(act_given, 1)
                given[0] += 1

            given = [0]

            def split_hi(Q, s0):
                act.wait_ge(raw_in[s0 % 4], (Q - s0) * 4 + (16 * (s0 // 4) + 16))
                for s in range(2):
                    i = (2 * s0 + s) % 4
                    if 2 * s0 + s >= 4:
                        act.wait_ge(half_used, Q * 2 + (s - 3))
                    act.activation(w_hi[i][:, :], raw[s0 % 4][:, 512 * s:512 * s + 512], ACT.Copy).then_inc(hi_ready, 1)

            def wait_step(l, name, k):
                act.wait_ge(step_done, N_STEPS * l + STEP_NO[(name, k)] + 1)

            def vec(*key):
                wait_mark(act, *key)

            vec("start", 0, 0)
            act.wait_ge(consts_in, 80)
            for j in range(8):
                act.wait_ge(x_in[j], 16)
                for t in range(2):
                    c = 2 * j + t
                    ins = act.activation(xg_hi[:, c, :], x_first[:, c, :], ACT.Copy, scale=col(0, R_NG + c))
                    if t:
                        give(ins)
                    else:
                        a(ins)

            def ext_fill(l, gi):
                if gi == 0:
                    act.wait_ge(hist_in, 16 * l + 16)
                else:
                    vec("diff", l, gi - 1)
                    a.settle()
                for t in range(2):
                    a(act.activation(ext[:, t, 0:HIST], hist[:, 2 * gi + t, 0:HIST], ACT.Copy))
                    last = act.activation(
                        ext[:, t, HIST + SEQ:EXT].rearrange("p (b t) -> p b t", t=HIST + TS)[:, :, 0:HIST],
                        hist[:, 2 * gi + t, HIST:].rearrange("p (b t) -> p b t", t=HIST), ACT.Copy)
                    if t == 0:
                        a(last)
                give(last)

            def hist_take(l, gi):
                vec("ext_full", l, gi)
                act.wait_ge(act_given, given[0])
                for t in range(2):
                    a(act.activation(hist[:, 2 * gi + t, 0:HIST], ext[:, t, SEQ:SEQ + HIST], ACT.Copy))
                    a(act.activation(
                        hist[:, 2 * gi + t, HIST:].rearrange("p (b t) -> p b t", t=HIST),
                        ext[:, t, HIST + SEQ:EXT].rearrange("p (b t) -> p b t", t=HIST + TS)[:, :, TS:], ACT.Copy))
                a.mark("hist", l, gi)

            def scalar_part(l, beat):
                if beat == 0:
                    act.wait_ge(rms_done, l + 1)
                    give(act.activation(rstd[:, :], rms_psum, ACT.Sqrt, scale=1.0 / D, bias=eps[:, :]))
                    marks[("rms_taken", l, 0)] = (act_given, given[0])
                if beat in (35, 38, 42, 46):
                    ext_fill(l, {35: 0, 38: 1, 42: 2, 46: 3}[beat])
                if beat in TAKEN_AT:
                    g = TAKEN_AT[beat]
                    if G_U <= g < G_BZ:
                        hist_take(l, g - G_U)
                    if G_BZ <= g < G_K or g >= G_CZ:
                        n, g0 = (BR_B, G_BZ) if g < G_K else (BR_C, G_CZ) if g < G_AZ else (BR_A, G_AZ)
                        i = 2 * (g - g0)
                        if g == G_CZ:
                            vec("roped", l, ("q_norm", 3))
                        vec("z", l, g)
                        give(act.activation(tc[:, :, :], ta[:, :, :], ACT.Sigmoid))
                        vec("gated", l, g)
                        give(act.activation(br_hi[n][:, i:i + 2, :], ta[:, :, :], ACT.Copy))
                for name, k, banks in STEPS.get(beat, ()):
                    if name == "gate":
                        vec("gate_in", l, 0)
                        a(act.activation(lev_e[:, :, :], cq[:, :, :], ACT.Abs))
                        a.settle()
                        a(act.activation(lev_e[:, :, :], lev_e[:, :, :], ACT.Exp, scale=-1.0))
                        a.settle()
                        give(act.activation(lev_e[:, :, :], lev_e[:, :, :], ACT.Ln, bias=1.0))
                    elif name == "v_turn_prompt":
                        wait_step(l, name, k)
                        a(act.activation(v_gla[:, 0:2, 256 * k:256 * k + 256],
                                         side[:, 3, :].rearrange("p (c n) -> p c n", c=2), ACT.Copy))
                        a.mark(name, l, k)
                    elif name == "v_turn_sample":
                        wait_step(l, name, k)
                        a(act.activation(v_gla[0:SMP, 2, 256 * k:256 * k + 256], side[0:SMP, 3, 0:256], ACT.Copy))
                        a.mark(name, l, k)
                    elif name == "k_turn":
                        wait_step(l, name, k)
                        for c in range(2):
                            a(act.activation(ko_tok[:, c, :], side[:, c, :], ACT.Copy))
                        a(act.activation(ko_tok[0:SMP, 2, :], side[0:SMP, 2, :], ACT.Copy))
                        a.settle()
                        a.mark(name, l, k)
                    elif name == "first_chunk":
                        wait_step(l, name, k)
                        a(act.activation(s1[:, :, :], side[:, 0:2, :].rearrange("p b (h n) -> p (b h) n", h=2), ACT.Copy))
                        a(act.activation(o_c[:, :, 0:P], side[:, 2:4, :].rearrange("p b (c n) -> p (b c) n", c=4),
                                         ACT.Copy))
                        a.mark(name, l, k)
                    elif name == "second_chunk":
                        wait_step(l, name, k)
                        a(act.activation(o_c[:, :, P:SEQ], side[:, 0:2, :].rearrange("p b (c n) -> p (b c) n", c=4),
                                         ACT.Copy))
                        a.mark(name, l, k)
                    elif name == "sample_gla" and k == 7:
                        wait_step(l, name, k)
                        a(act.activation(o_c[:, :, SEQ:TOK], side[:, 3, :].rearrange("p (c n) -> p c n", c=8), ACT.Copy))
                        a.settle()
                        a.mark(name, l, k)
                    elif name == "gla_norm":
                        wait_step(l, name, k)
                        if k:
                            vec("gla_scaled", l, 0)
                        give(act.activation(tb[:, :, :], side[:, 0:2, 0:TOK], ACT.Sqrt, scale=1.0 / DV, bias=eps[:, :]))
                        marks[("gla_ms", l, k)] = (act_given, given[0])
                    elif name in ("k_norm", "q_norm"):
                        wait_step(l, name, k)
                        if name == "k_norm":
                            vec("gla_scaled", l, 1)
                        give(act.activation(tb[:, :, :], side[:, 2:4, 0:TOK], ACT.Sqrt, scale=1.0 / HD, bias=eps[:, :]))
                        marks[("head_ms", l, (name, k))] = (act_given, given[0])
                        vec("normed", l, (name, k))
                        for q in range(4):
                            ins = act.activation(tc[32 * q:32 * q + 32, :, :], ta[32 * (q ^ 1):32 * (q ^ 1) + 32, :, :],
                                                 ACT.Copy)
                            if q == 3:
                                give(ins)
                            else:
                                a(ins)
                    elif name == "kv_turn":
                        wait_step(l, name, k)
                        act.wait_ge(s2_out, 16 * l + 16)
                        a(act.activation(v_tok[:, 0:2, :], side[:, 2, :].rearrange("p (c n) -> p c n", c=2), ACT.Copy))
                        a(act.activation(v_tok[0:SMP, 2, :], side[0:SMP, 3, 0:256], ACT.Copy))
                        a.mark(name, l, k)
                    elif name == "scores":
                        p = probs[k % 2]
                        vec("masked", l, k)
                        for i in range(4):
                            lo, n = ((0, 256), (384, 256), (256, 128), (640, 128))[i]
                            a(act.activation(p[:, lo:lo + n], p[:, lo:lo + n], ACT.Exp, bias=small[:, 4 + i:5 + i],
                                             accum_out=small[:, 12 + i:13 + i]))
                        give(act.activation(small[:, 20:24], small[:, 8:12], ACT.Exp))
                    elif name == "p_turn":
                        wait_step(l, name, k)
                        a(act.activation(probs[k % 2][:, :].rearrange("p (h k) -> p h k", h=2),
                                         side[:, banks[0]:banks[0] + 2, 0:384], ACT.Copy))
                        a.mark(name, l, k)
                    elif name == "pv":
                        wait_step(l, name, k)
                        a(act.activation(o_ab[:, k, 0:SEQ].rearrange("p (c t) -> p c t", c=2),
                                         side[:, banks[0]:banks[0] + 2, 384:512], ACT.Copy))
                        a.mark(name, l, k)
                    elif name == "sample_scores":
                        p = probs[k % 2]
                        vec("sample_masked", l, k)
                        for i in range(2):
                            a(act.activation(p[:, 192 * i:192 * i + 192], p[:, 192 * i:192 * i + 192], ACT.Exp,
                                             bias=small[:, 4 + i:5 + i], accum_out=small[:, 12 + i:13 + i]))
                        give(act.activation(small[:, 20:22], small[:, 8:10], ACT.Exp))
                    elif name == "sample_p_turn":
                        wait_step(l, name, k)
                        s3 = side[:, banks[0], :].rearrange("p (b n) -> p b n", b=4)
                        p3 = probs[k % 2][:, 0:512].rearrange("p (b n) -> p b n", b=4)
                        a(act.activation(p3[:, 0:2, :], s3[:, 0:2, :], ACT.Copy))
                        a(act.activation(p3[0:SMP, 2:4, :], s3[0:SMP, 2:4, :], ACT.Copy))
                        a.mark(name, l, k)
                    elif name == "sample_pv" and k == 3:
                        wait_step(l, name, k)
                        a(act.activation(o_ab[:, :, SEQ:TOK], side[:, 2, :].rearrange("p (c n) -> p c n", c=8), ACT.Copy))
                        a.mark(name, l, k)
                for k in range(1, 8):
                    if beat == 17 + 2 * k:
                        B = LEVELS[k - 1]
                        e4, n = segs(lev_e, B)
                        vec("level_gap", l, k)
                        for h in range(GH):
                            a(act.activation(e4[:, h, :, 0:B], e4[:, h, :, 0:B], ACT.Exp, scale=-1.0))
                            ins = act.activation(e4[:, h, :, B:2 * B], e4[:, h, :, B:2 * B], ACT.Exp)
                            if h == GH - 1:
                                give(ins)
                            else:
                                a(ins)
                if beat == 34:
                    vec("level", l, 7)
                    a(act.activation(edge[:, :, 0:2], cb[:, :, 0:SEQ].rearrange("p h (a b) -> p h a b", b=P)[:, :, :, P - 1],
                                     ACT.Exp))
                    a(act.activation(edge[:, :, 2:], cb[:, :, SEQ:TOK].rearrange("p h (a b) -> p h a b", b=TS)[:, :, :, TS - 1],
                                     ACT.Exp))
                    give(act.activation(lev_e[:, :, :], cb[:, :, :], ACT.Exp))
                    vec("end_gap", l, 0)
                    give(act.activation(lev_e[:, :, :], lev_e[:, :, :], ACT.Exp))
                for k in range(2):
                    if beat == 67 + 2 * k:
                        if k:
                            wait_step(l, "gla_norm", 0)
                        a(act.activation(squares[:, :, :], o_c[:, 4 * k:4 * k + 4, :], ACT.Square))
                        a.mark("squares", l, k)
                for name, k, at in [("k_norm", 0, 69)] + [("q_norm", k, 77 + 4 * k) for k in range(4)]:
                    if beat == at:
                        s, n = marks[("taken", l, G_K if name == "k_norm" else G_Q + k)]
                        act.wait_ge(s, n)
                        if name == "q_norm":
                            vec("roped", l, ("q_norm", k - 1) if k else ("k_norm", 0))
                        a(act.activation(tc[:, :, :], ta[:, :, :], ACT.Square))
                        a.mark("head_squares", l, (name, k))
            def mix_body(l, i):
                Q0 = BEATS * l + IN_BEATS
                G0 = GROUPS * l + 1 + N_IN
                b = 0
                for jj in range(2):
                    for n in range(3):
                        for part in range(6):
                            split_hi(i * 36 + (Q0 + b + 2), Q0 + b + 2)
                            b += 1
                            if part == 3:
                                act.wait_ge(main_free, i * 12 + (G0 + 6 * jj + 2 * n + 1))
                                act.activation(tb[:, :, :], ta[:, :, :], ACT.Sigmoid).then_inc(act_given, 1)

            for l in range(DEPTH):
                last_layer = l == DEPTH - 1
                for beat in range(IN_BEATS):
                    Q = BEATS * l + beat
                    if l == 0 and beat == 0:
                        split_hi(0, 0)
                        split_hi(1, 1)
                    split_hi(Q + 2, Q + 2)
                    scalar_part(l, beat)
                with act.Fori(0, 4) as i:
                    mix_body(l, i)
                given[0] += 24
                Q0 = BEATS * l + IN_BEATS + MIX_BEATS
                with act.Fori(0, 3 if last_layer else 4) as i:
                    for b in range(8):
                        split_hi(i * 8 + (Q0 + b + 2), Q0 + b + 2)
                if last_layer:
                    for b in range(6):
                        split_hi(24 + Q0 + b + 2, 24 + Q0 + b + 2)

        @block.sync
        def _(sp):
            def load(Q, s0):
                if s0 >= 4:
                    sp.wait_ge(lo_ready, Q * 2 - 6)
                sp.dma_start(raw[s0 % 4][:, :], ins["w_stream"][bass.ds(Q, 1)].rearrange("a p n -> (a p) n")
                             if not isinstance(Q, int) else ins["w_stream"][Q]).then_inc(raw_in[s0 % 4], 16)

            for Q in range(4):
                load(Q, Q)
            total = BEATS * DEPTH
            with sp.Fori(1, total // 4) as i:
                for s in range(4):
                    load(i * 4 + s, 4 + s)
            for Q in range(total // 4 * 4, total):
                load(Q, Q)

        @block.gpsimd
        def _(pool):
            def load(dst, src, s):
                pool.dma_start(dst, src).then_inc(s, 16)

            def store_y(l, j):
                pool.wait_ge(main_free, GROUPS * l + 1 + N_IN + 6 * PAIRS + j + 1)
                load((outs["y"] if l == DEPTH - 1 else ins["y_mid"])[j], (ta, tb)[j % 2][:, :, :], y_out[j % 2])

            for j in range(8):
                load(x_first[:, 2 * j:2 * j + 2, :], ins["x_pairs"][j], x_in[j])
                if j == 0:
                    load(const[:, :], ins["consts"], consts_in)
                    load(par[:, :, :], ins["params"], consts_in)
            load(amask_p[:, :], ins["amask_p"], consts_in)
            load(amask_s[:, :], ins["amask_s"], consts_in)
            load(gmask_f[:, :, :], ins["gmask"], consts_in)
            for l in range(DEPTH):
                if l:
                    pool.wait_ge(half_used, last_half(l - 1, IN_BEATS + MIX_BEATS - 1))
                load(w_gate[0:RANK, :], ins["w_gate"][l], w_gate_in)
                load(w_pool[:, :, :], ins["w_pool"][l], w_pool_in)
                if l:
                    pool.wait_ge(half_used, last_half(l - 1, BEATS - 1))
                else:
                    wait_mark(pool, "sq_sum", 0, 0)
                load(hist[:, :, :], ins["hist"][l], hist_in)
                load(outs["k_window"][l], ins["cache_k_tok"][l, :, TS:WINDOW, :], window_out)
                load(outs["new_v_s"][l, :, 0:WINDOW - TS, :], ins["cache_v_tok"][l, :, TS:WINDOW, :], window_out)
                wait_mark(pool, "carry", l, 0)
                for k in range(2):
                    load(state[:, k, :, :], ins["state"][l, k], state_in[k])
                s, n = marks[("hist", l, 3)]
                pool.wait_ge(s, n)
                load(outs["hist"][l], hist[:, :, :], hist_out)
                wait_mark(pool, "second_state", l, 0)
                load(outs["state_p"][l], s1[:, :, :], s2_out)
                for k in range(8):
                    wait_mark(pool, "sample_state", l, k)
                    load(outs["state_s"][l, k], state[:, k % 2, :, :], state_out[k % 2])
                    if k < 6:
                        pool.wait_ge(state_out[k % 2], 16 * (4 * l + k // 2 + 1))
                        load(state[:, k % 2, :, :], ins["state"][l, k + 2], state_in[k % 2])
                for i in range(2):
                    pool.wait_ge(state_out[i], 64 * l + 64)
                load(cache_k[:, :, :, :], ins["cache_k"][l], caches_in)
                load(cache_v[:, :, :], ins["cache_v"][l], caches_in)
                wait_mark(pool, "roped", l, ("k_norm", 0))
                load(outs["k_new"][l], k_a[:, :, P:TOK], kv_out)
                s, n = marks[("taken", l, G_V)]
                pool.wait_ge(s, n)
                load(outs["v_new"][l], tb[:, :, P:SEQ], kv_out)
                wait_mark(pool, "kv_turn", l, 0)
                load(outs["new_v_s"][l, :, WINDOW - TS:WINDOW, :], v_tok[0:SMP, 2, :], kv_out)
                for j in range(8):
                    slot = (ta, tb)[j % 2]
                    if j < 2:
                        wait_mark(pool, "merged", l, 0)
                    else:
                        pool.wait_ge(y_out[j % 2], 16 * (4 * l + (j - 2) // 2 + 1))
                        if l < DEPTH - 1:
                            wait_mark(pool, "xg", l + 1, j - 2)
                    load(slot[:, :, :], ins["x_pairs"][j] if l == 0 else ins["y_mid"][j], res_in[j % 2])
                    if j >= 1:
                        store_y(l, j - 1)
                store_y(l, 7)
                for i in range(2):
                    pool.wait_ge(y_out[i], 64 * (l + 1))
            pool.wait_ge(hist_out, 16 * DEPTH)
            pool.wait_ge(s2_out, 16 * DEPTH)
            pool.wait_ge(kv_out, 48 * DEPTH)
            pool.wait_ge(window_out, 32 * DEPTH)

        @block.tensor
        def _(pe):
            def free_banks(l, step):
                i = STEP_NO[step]
                for b in BANKS[step]:
                    for m in range(i - 1, i - 1 - N_STEPS, -1):
                        s = ORDER[m % N_STEPS]
                        if b in BANKS[s]:
                            ll = l + (m // N_STEPS)
                            if ll >= 0 and s in READ_BY:
                                for key in READ_BY[s]:
                                    wait_mark(pe, key[0], ll, key[1])
                            break

            READ_BY = {("gate", 0): [("gate_in", 0)], ("k_turn", 0): [("k_turn", 0)],
                       ("first_chunk", 0): [("first_chunk", 0)],
                       ("second_chunk", 0): [("second_chunk", 0), ("second_state", 0)],
                       ("kv_turn", 0): [("kv_turn", 0)], ("k_norm", 0): [("head_ms", ("k_norm", 0))]}
            for k in range(8):
                READ_BY[("level", k)] = [("att", k)]
                READ_BY[("sample_gla", k)] = [("sample_state", k)]
                READ_BY[("scores", k)] = [("masked", k)]
                READ_BY[("p_turn", k)] = [("p_turn", k)]
                READ_BY[("pv", k)] = [("pv", k)]
            READ_BY[("sample_gla", 7)].append(("sample_gla", 7))
            for k in range(4):
                READ_BY[("v_turn_prompt", k)] = [("v_turn_prompt", k)]
                READ_BY[("v_turn_sample", k)] = [("v_turn_sample", k)]
                READ_BY[("pool", k)] = [("pooled", k)]
                READ_BY[("q_norm", k)] = [("head_ms", ("q_norm", k))]
                READ_BY[("sample_scores", k)] = [("sample_masked", k)]
                READ_BY[("sample_p_turn", k)] = [("sample_p_turn", k)]
            READ_BY[("sample_pv", 3)] = [("sample_pv", 3)]
            for k in range(2):
                READ_BY[("gla_norm", k)] = [("gla_ms", k)]

            def mm(out, lhsT, rhs, start=True, stop=True):
                return pe.matmul(out, lhsT, rhs, start=start, stop=stop)

            def turn(out, src):
                return pe.transpose(out, src, ident[0:src.shape[0], 0:src.shape[0]])

            def block_products(Q, s0, G, tiles, hi, lo, k0, first, last, narrow=False):
                base = 2 * (G % 2)
                for s in range(2):
                    i = (2 * s0 + s) % 4
                    pe.wait_ge(lo_ready, Q * 2 + (s + 1))
                    nk = 4 if narrow else 2
                    w = 128 if narrow else 256
                    for kk in range(nk):
                        k = k0 + nk * s + kk
                        for t in range(tiles):
                            c = kk * w + t * P
                            out = main[:, base + t, 0:TOK]
                            st = first and s == 0 and kk == 0
                            sp_ = last and s == 1 and kk == nk - 1
                            mm(out, w_hi[i][:, c:c + P], hi[:, k, :], st, False)
                            mm(out, w_hi[i][:, c:c + P], lo[:, k, :], False, False)
                            ins_ = mm(out, w_lo[i][:, c:c + P], hi[:, k, :], False, sp_)
                    ins_.then_inc(half_used, 1)

            def side_step(l, name, k, banks):
                free_banks(l, (name, k))
                wm = lambda *key: wait_mark(pe, *key)
                if name == "gate":
                    wm("lr", l, 0)
                    wm("rms_taken", l, 0)
                    pe.wait_ge(w_gate_in, 16 * l + 16)
                    for h in range(GH):
                        last = mm(side[:, h, 0:TOK], w_gate[0:RANK, DK * h:DK * h + DK], ta[0:RANK, 0, :])
                elif name == "level":
                    if k == 0:
                        wm("taken", l, G_CV - 1)
                        wm("decay", l, 0)
                        kk, qq = ck, cq
                    else:
                        wm("level", l, k)
                        kk, qq = lev_k, lev_q
                    for c in range(2):
                        for h in range(GH):
                            last = mm(side[:, c, P * h:P * h + P], kk[:, h, P * c:P * c + P], qq[:, h, P * c:P * c + P])
                    if k <= 3:
                        for h in range(GH):
                            last = mm(side[0:SMP, 2, SMP * h:SMP * h + SMP], kk[:, h, SEQ:TOK], qq[:, h, SEQ:TOK])
                elif name == "v_turn_prompt":
                    wm("taken", l, G_CV + k)
                    for c in range(2):
                        for t in range(2):
                            last = turn(side[:, 3, 256 * c + P * t:256 * c + P * t + P],
                                        o_c[:, 2 * k + t, P * c:P * c + P])
                elif name == "v_turn_sample":
                    for t in range(2):
                        last = turn(side[0:SMP, 3, P * t:P * t + P], o_c[:, 2 * k + t, SEQ:TOK])
                elif name == "k_turn":
                    wm("carry", l, 0)
                    for h in range(GH):
                        for c in range(2):
                            turn(side[:, c, DK * h:DK * h + DK], lev_k[:, h, P * c:P * c + P])
                        last = turn(side[0:SMP, 2, DK * h:DK * h + DK], lev_k[:, h, SEQ:TOK])
                elif name == "pool":
                    wm("diff", l, k)
                    pe.wait_ge(w_pool_in, 16 * l + 16)
                    for t in range(2):
                        for c in range(2):
                            last = mm(side[:, 2 + t, 0:TOK], w_pool[:, 2 * k + c, P * t:P * t + P], diff[:, c, :],
                                      c == 0, c == 1)
                elif name == "first_chunk":
                    wm("k_turn", l, 0)
                    wm("v_turn_sample", l, 3)
                    wm("att", l, 7)
                    for h in range(GH):
                        mm(side[:, h // 2, 256 * (h % 2):256 * (h % 2) + 256], ko_tok[:, 0, DK * h:DK * h + DK],
                           v_gla[:, 0, DV * h:DV * h + DV])
                    for c in range(8):
                        last = mm(side[:, 2 + c // 4, P * (c % 4):P * (c % 4) + P], v_gla[:, 0, P * c:P * c + P],
                                  att_p[:, 0, P * (c // 2):P * (c // 2) + P])
                elif name == "second_chunk":
                    wm("first_chunk", l, 0)
                    for c in range(8):
                        h, out = c // 2, side[:, c // 4, P * (c % 4):P * (c % 4) + P]
                        mm(out, v_gla[:, 1, P * c:P * c + P], att_p[:, 1, P * h:P * h + P], True, False)
                        mm(out, s1[:, h, P * (c % 2):P * (c % 2) + P], lev_q[:, h, P:SEQ], False, True)
                    for h in range(GH):
                        last = mm(side[:, 2 + h // 2, 256 * (h % 2):256 * (h % 2) + 256],
                                  ko_tok[:, 1, DK * h:DK * h + DK], v_gla[:, 1, DV * h:DV * h + DV])
                elif name == "sample_gla":
                    h, half = divmod(k, 2)
                    pe.wait_ge(state_in[k % 2], 64 * l + 16 * (k // 2) + 16)
                    wm("k_sel", l, k)
                    for t in range(2):
                        c = 2 * h + t
                        for b in range(4):
                            n = 32 * half + TS * b
                            out = side[:, 3, SMP * c + n:SMP * c + n + TS]
                            mm(out, v_gla[0:SMP, 2, P * c:P * c + P], att_s[0:SMP, SMP * h + n:SMP * h + n + TS],
                               True, False)
                            mm(out, state[:, k % 2, b, P * t:P * t + P], lev_q[:, h, SEQ + n:SEQ + n + TS], False, True)
                    for b in range(4):
                        last = mm(side[:, b // 2, 256 * (b % 2):256 * (b % 2) + 256], k_sel[0:SMP, b, :],
                                  v_gla[0:SMP, 2, DV * h:DV * h + DV])
                elif name == "gla_norm":
                    wm("squares", l, k)
                    for i in range(2):
                        for t in range(2):
                            last = mm(side[:, i, 0:TOK], ones[:, :], squares[:, 2 * i + t, :], t == 0, t == 1)
                elif name in ("k_norm", "q_norm"):
                    wm("head_squares", l, (name, k))
                    for t in range(2):
                        last = mm(side[:, 2 + t, 0:TOK], head_ones, tc[:, t, :])
                elif name == "kv_turn":
                    wm("taken", l, G_V)
                    for t in range(2):
                        for c in range(2):
                            turn(side[:, 2, 256 * c + P * t:256 * c + P * t + P], tb[:, t, P * c:P * c + P])
                        last = turn(side[0:SMP, 3, P * t:P * t + P], tb[:, t, SEQ:TOK])
                elif name == "scores":
                    wm("roped", l, ("q_norm", k // 2))
                    kt = k // 4
                    for i in range(2):
                        rows = slice(HD * i, HD * i + HD)
                        mm(side[:, banks[i], 0:256], q_a[rows, k, P:SEQ], k_a[rows, kt, 0:SEQ])
                        last = mm(side[:, banks[i], 256:384], q_a[rows, k, 0:P], k_a[rows, kt, 0:P])
                elif name == "p_turn":
                    wm("probs", l, k)
                    for i in range(2):
                        for c in range(3):
                            last = turn(side[:, banks[i], P * c:P * c + P],
                                        probs[k % 2][:, 384 * i + P * c:384 * i + P * c + P])
                elif name == "pv":
                    wm("p_turn", l, k)
                    wm("kv_turn", l, 0)
                    p = probs[k % 2]
                    for i in range(2):
                        kv = 2 * (k // 4) + i
                        rows = slice(HD * i, HD * i + HD)
                        vc = slice(HD * kv, HD * kv + HD)
                        n = 384 * i
                        early, late = side[rows, banks[0], 384:512], side[rows, banks[1], 384:512]
                        mm(late, v_tok[:, 0, vc], p[:, n:n + P], True, False)
                        mm(late, v_tok[:, 1, vc], p[:, n + P:n + 2 * P], False, True)
                        last = mm(early, v_tok[:, 0, vc], p[:, n + 2 * P:n + 3 * P])
                elif name == "sample_scores":
                    pe.wait_ge(caches_in, 32 * l + 32)
                    for b in range(2):
                        for i in range(2):
                            qs = q_s[:, i, 2 * k + b, :, :, :].rearrange("p j g t -> p (j g t)")
                            out = side[64 * i:64 * i + 64, banks[0], 192 * b:192 * b + 192]
                            mm(out[:, 0:WINDOW], qs, cache_k[:, i, 2 * k + b, :])
                            last = mm(out[:, WINDOW:], qs, k_a[:, i, SEQ:TOK])
                elif name == "sample_p_turn":
                    wm("sample_probs", l, k)
                    p = probs[k % 2]
                    for b in range(2):
                        turn(side[:, banks[0], P * b:P * b + P], p[:, 192 * b:192 * b + WINDOW])
                        last = turn(side[0:SMP, banks[0], 256 + P * b:384 + P * b], p[:, 192 * b + WINDOW:192 * b + 192])
                elif name == "sample_pv":
                    wm("sample_p_turn", l, k)
                    p = probs[k % 2]
                    for b in range(2):
                        for kv in range(KVH):
                            rows = slice(HD * (kv % 2), HD * (kv % 2) + HD)
                            vc = slice(HD * kv, HD * kv + HD)
                            o4 = side[rows, 2, :].rearrange("p (j t) -> p j t", j=8)
                            n = TS * (2 * k + b)
                            out = o4[:, 4 * (kv // 2):4 * (kv // 2) + 4, n:n + TS]
                            mm(out, cache_v[:, 2 * k + b, vc], p[:, P * b + 32 * kv:P * b + 32 * kv + 32], True, False)
                            last = mm(out, v_tok[0:SMP, 2, vc], p[0:SMP, 256 + P * b + 32 * kv:256 + P * b + 32 * kv + 32],
                                      False, True)
                last.then_inc(step_done, 1)

            def wait_main(G0, value):
                if G0 >= 2:
                    pe.wait_ge(main_free, value)

            for l in range(DEPTH):
                for beat in range(IN_BEATS):
                    Q = BEATS * l + beat
                    if beat < LR_BEATS:
                        G = GROUPS * l
                        if beat == 0:
                            wait_main(G, G - 1)
                        for j in range(4 * beat, 4 * beat + 4):
                            wait_mark(pe, "xg", l, j)
                        block_products(Q, Q, G, 1, xg_hi, xg_lo, 8 * beat, beat == 0, beat == 1, narrow=True)
                    else:
                        g, part = divmod(beat - LR_BEATS, 4)
                        G = GROUPS * l + 1 + g
                        if part == 0:
                            wait_main(G, G - 1)
                        block_products(Q, Q, G, 2, xg_hi, xg_lo, 4 * part, part == 0, part == 3)
                    if beat == 0:
                        wait_mark(pe, "sq_sum", l, 0)
                        if l:
                            free_banks(l, ORDER[0])
                        mm(rms_psum, ones[:, :], sq_sum[:, :]).then_inc(rms_done, 1)
                    for name, k, banks in STEPS.get(beat, ()):
                        side_step(l, name, k, banks)
                wait_mark(pe, "branches", l, 0)
                Q0 = BEATS * l + IN_BEATS
                G0 = GROUPS * l + 1 + N_IN
                with pe.Fori(0, PAIRS // 2) as i:
                    b = 0
                    G = G0
                    for jj in range(2):
                        for n in range(3):
                            pe.wait_ge(main_free, i * 12 + (G - 1))
                            for part in range(4):
                                block_products(i * 36 + (Q0 + b), Q0 + b, G, 2, xg_hi, xg_lo, 4 * part,
                                               part == 0, part == 3)
                                b += 1
                            G += 1
                            pe.wait_ge(main_free, i * 12 + (G - 1))
                            for part in range(2):
                                block_products(i * 36 + (Q0 + b), Q0 + b, G, 2, br_hi[n], br_lo[n], 4 * part,
                                               part == 0, part == 1)
                                b += 1
                            G += 1
                Q0 += MIX_BEATS
                G0 += 6 * PAIRS
                wait_mark(pe, "merged", l, 0)
                with pe.Fori(0, PAIRS // 2) as i:
                    for jj in range(2):
                        pe.wait_ge(main_free, i * 2 + (G0 + jj - 1))
                        for part in range(4):
                            b = 4 * jj + part
                            block_products(i * 8 + (Q0 + b), Q0 + b, G0 + jj, 2, mg_hi, mg_lo, 4 * part,
                                           part == 0, part == 3)


def _constants():
    import numpy as np
    p = np.arange(P)
    c = np.zeros((P, C_END), np.float32)
    pos = np.concatenate([np.arange(SEQ), np.tile(PAST + np.arange(TS), NB)]).astype(np.float32)
    inv = np.power(10000.0, -np.arange(HD // 2) * (2.0 / HD)).astype(np.float32)
    ang = (pos[None, :] * inv[p % (HD // 2)][:, None]).astype(np.float32)
    sign = np.where(p % HD < HD // 2, -1.0, 1.0)[:, None]
    c[:, C_COS:C_COS + TOK] = np.cos(ang.astype(np.float64))
    c[:, C_SIN:C_SIN + TOK] = sign * np.sin(ang.astype(np.float64))
    c[:, C_IDENT:C_IDENT + P] = np.eye(P)
    c[:, C_BLOCK:C_BLOCK + P] = p[:, None] // HD == p[None, :] // HD
    t = np.arange(TOK)
    c[:, C_KEEP:C_KEEP + TOK] = np.where(t < SEQ, t % P != 0, t % TS != 0)
    for g in range(4):
        c[:, C_INVC + 16 * g:C_INVC + 16 * g + 16] = 1.0 / np.minimum(2 << g, np.arange(16) + 1)
    c[:, C_BSEL:C_BSEL + NB] = p[:, None] // TS == np.arange(NB)[None, :]
    far = np.float32(-1e30)
    i, j = p[:, None], p[None, :]
    am = np.concatenate([np.where(j >= i, 0, far), np.where(j <= i, 0, far)], axis=1)
    t = p[:, None] % TS
    s = np.arange(SMP)[None, :]
    new = [np.where((s // TS == b) & (s % TS <= t), 0, far) for b in range(NB)]
    asm = np.concatenate([np.where(j >= t, 0, far)] + new, axis=1)
    gm = np.zeros((P, 8, P), np.float32)
    gm[:, 0] = i == j
    for k, B in enumerate(LEVELS):
        gm[:, k + 1] = (i // (2 * B) == j // (2 * B)) & (i % (2 * B) < B) & (j % (2 * B) >= B)
    return c, am, asm, gm


def kernel(**inputs):
    import ml_dtypes
    import numpy as np
    import concourse.bacc as bacc
    from concourse.bass_utils import run_bass_kernel_spmd

    x = {n: np.asarray(a) for n, a in inputs.items()}
    pair_heads = [h for j in range(8) for h in (8 * (j // 4) + j % 4, 8 * (j // 4) + j % 4 + 4)]
    head_rows = np.concatenate([np.arange(HD * h, HD * h + HD) for h in pair_heads])
    cols = {"a_q": head_rows, "a_k": 1024 + np.arange(256), "a_v": 1280 + np.arange(256), "a_z": 1536 + head_rows,
            "b_u": 2560 + np.arange(1024), "b_z": 3584 + np.arange(1024), "c_q": 4608 + np.arange(512),
            "c_k": 5120 + np.arange(512), "c_v": 5632 + np.arange(1024), "c_z": 6672 + np.arange(1024)}
    order = np.concatenate([cols[n] for n in ("c_q", "c_k", "c_v", "b_u", "b_z", "a_k", "a_v", "a_q", "c_z", "a_z")])
    lr0, gate0 = 6656, 7696
    w = np.zeros((DEPTH, BEATS, P, 1024), np.float32)
    for l in range(DEPTH):
        win, wbr, wout = x["w_in"][l], x["w_branch"][l], x["w_out"][l]
        lr = w[l, 0:2].reshape(2, P, 8, 128)
        lr[:, :, :, 0:RANK] = win[:, lr0:lr0 + RANK].reshape(2, 8, P, RANK).transpose(0, 2, 1, 3)
        m = win[:, order].reshape(4, 4, P, N_IN, 256)
        w[l, 2:IN_BEATS] = m.transpose(3, 0, 2, 1, 4).reshape(4 * N_IN, P, 1024)
        mix = w[l, IN_BEATS:IN_BEATS + MIX_BEATS].reshape(PAIRS, 3, 6, P, 4, 256)
        gates = win[:, gate0:].reshape(4, 4, P, 3, PAIRS, 256)
        mix[:, :, 0:4] = gates.transpose(4, 3, 0, 2, 1, 5)
        for n in range(3):
            rows = wbr[n][head_rows] if n == BR_A else wbr[n]
            mix[:, n, 4:6] = rows.reshape(2, 4, P, PAIRS, 256).transpose(3, 0, 2, 1, 4)
        w[l, IN_BEATS + MIX_BEATS:] = wout.reshape(4, 4, P, PAIRS, 256).transpose(3, 0, 2, 1, 4).reshape(32, P, 1024)

    def cm(a, n):
        return a.reshape(a.shape[:-1] + (n, P)).swapaxes(-1, -2)

    tok = np.concatenate([x["x_prompt"][0], x["x_sample"].reshape(SMP, D)], axis=0)
    par = np.zeros((P, DEPTH, R_END), np.float32)
    for l in range(DEPTH):
        par[:, l, R_NG:R_NG + 16] = cm(x["norm_g"][l], 16)
        par[:, l, R_QG] = np.tile(x["q_norm_g"][l], 2)
        par[:, l, R_KG] = np.tile(x["k_norm_g"][l], 2)
        par[:, l, R_SINK:R_SINK + 16] = x["sinks"][l][pair_heads][None, :]
        par[:, l, R_SSINK] = np.repeat(x["sinks"][l], TS)
        par[:, l, R_PS:R_PS + 8] = cm(x["pool_scale"][l], 8)
        par[:, l, R_BG:R_BG + 4] = cm(x["b_gate"][l], 4)
        par[:, l, R_GG:R_GG + 2] = cm(x["gla_norm_g"][l], 2)
    hist = np.zeros((DEPTH, P, 8, 1 + NB, HIST), np.float32)
    hist[:, :, :, 1:] = x["state_pool"].reshape(DEPTH, NB, HIST, 8, P).transpose(0, 4, 3, 1, 2)
    consts, amask_p, amask_s, gmask = _constants()
    ck = x["cache_a_k"].reshape(DEPTH, NB, WINDOW, 2, P)
    feeds = {
        "w_stream": w.reshape(DEPTH * BEATS, P, 1024),
        "x_pairs": tok.T.reshape(PAIRS, 2, P, TOK).transpose(0, 2, 1, 3),
        "consts": consts,
        "amask_p": amask_p.astype(ml_dtypes.bfloat16),
        "amask_s": amask_s.astype(ml_dtypes.bfloat16),
        "gmask": gmask,
        "params": par,
        "hist": hist.reshape(DEPTH, P, 8, (1 + NB) * HIST),
        "w_pool": x["w_pool"].reshape(DEPTH, 4, 2, P, 256).transpose(0, 3, 1, 2, 4).reshape(DEPTH, P, 8, 256),
        "w_gate": x["w_gate_lr"],
        "state": x["state_gla"].reshape(DEPTH, 2, 4, GH, DK, DV).transpose(0, 3, 1, 4, 2, 5).reshape(DEPTH, 8, DK, 4, DV),
        "cache_k": ck.transpose(0, 4, 3, 1, 2),
        "cache_v": x["cache_a_v"].reshape(DEPTH, NB, WINDOW, 256).transpose(0, 2, 1, 3),
        "cache_k_tok": x["cache_a_k"].reshape(DEPTH, NB, WINDOW, 256),
        "cache_v_tok": x["cache_a_v"].reshape(DEPTH, NB, WINDOW, 256),
    }
    shapes = {"y": (PAIRS, P, 2, TOK), "k_new": (DEPTH, P, 2, P + SMP), "v_new": (DEPTH, P, 2, P),
              "k_window": (DEPTH, NB, WINDOW - TS, 256), "new_v_s": (DEPTH, NB, WINDOW, 256),
              "hist": (DEPTH, P, 8, (1 + NB) * HIST), "state_p": (DEPTH, DK, GH, DV), "state_s": (DEPTH, 8, DK, 4, DV)}
    nc = bacc.Bacc("TRN2", target_bir_lowering=False, num_devices=1)
    arrays = {f"in_{n}": np.ascontiguousarray(a) for n, a in feeds.items()}
    ins = {n: nc.dram_tensor(f"in_{n}", a.shape, mybir.dt.from_np(a.dtype), kind="ExternalInput").ap()
           for n, a in feeds.items()}
    ins["y_mid"] = nc.dram_tensor("y_mid", (PAIRS, P, 2, TOK), F32, kind="Internal").ap()
    outs = {n: nc.dram_tensor(f"out_{n}", s, F32, kind="ExternalOutput").ap() for n, s in shapes.items()}
    trunk(nc, ins, outs)
    r = run_bass_kernel_spmd(nc, [arrays], core_ids=[0]).results[0]
    o = {n: np.asarray(r[f"out_{n}"]).reshape(s) for n, s in shapes.items()}

    y = o["y"].transpose(0, 2, 1, 3).reshape(D, TOK).T
    kn = o["k_new"].transpose(0, 3, 2, 1).reshape(DEPTH, P + SMP, KVH, HD)
    vn = o["v_new"].transpose(0, 3, 2, 1).reshape(DEPTH, 1, P, KVH, HD)
    kw = np.concatenate([o["k_window"].reshape(DEPTH, NB, WINDOW - TS, KVH, HD),
                         kn[:, P:].reshape(DEPTH, NB, TS, KVH, HD)], axis=2)
    hs = o["hist"].reshape(DEPTH, P, 8, 1 + NB, HIST).transpose(0, 3, 4, 2, 1).reshape(DEPTH, 1 + NB, HIST, BRANCH)
    ss = o["state_s"].reshape(DEPTH, GH, 2, DK, 4, DV).transpose(0, 2, 4, 1, 3, 5).reshape(DEPTH, NB, GH, DK, DV)
    return (y[None, :SEQ], y[SEQ:].reshape(NB, TS, D),
            kn[:, None, :P], vn, hs[:, 0:1], o["state_p"].transpose(0, 2, 1, 3)[:, None],
            kw, o["new_v_s"].reshape(DEPTH, NB, WINDOW, KVH, HD), hs[:, 1:], ss)
```

```python
from contextlib import ExitStack

import concourse.bass as bass
from concourse import mybir

F32 = mybir.dt.float32
F32R = mybir.dt.float32r
BF16 = mybir.dt.bfloat16
U8 = mybir.dt.uint8
ALU = mybir.AluOpType
ACT = mybir.ActivationFunctionType
AX = mybir.AxisListType

P = 128
DEPTH = 2
D = 2048
BRANCH = 1024
SEQ = 256
NB = 8
TS = 8
SMP = NB * TS
TOK = SEQ + SMP
KT_D = D // P
WINDOW = 128
HEADS = 16
KVH = 4
HD = 64
GH = 4
DK = 128
DV = 256
RANK = 16
HIST = 15
PAST = 2048
EPS = 1e-6
LEVELS = [1, 2, 4, 8, 16, 32, 64]

G_CQ, G_CK, G_CV, G_U, G_BZ, G_K, G_V, G_Q, G_CZ, G_AZ = 0, 2, 4, 8, 12, 16, 17, 18, 22, 26
N_IN = 30
LR_AT, LR_BEATS = 8, 2
IN_BEATS = LR_BEATS + 4 * N_IN
PAIRS = D // 256
MIX_BEATS = PAIRS * 3 * 6
OUT_BEATS = PAIRS * 4
BEATS = IN_BEATS + MIX_BEATS + OUT_BEATS
GROUPS = 1 + N_IN + PAIRS * 6 + PAIRS
BR_A, BR_B, BR_C = 0, 1, 2
MIX_ORDER = (BR_B, BR_C, BR_A)
LN_EXP_TABLE = 6
STATES = 3


def first_beat(g):
    return 4 * g if g < LR_AT // 4 else LR_BEATS + 4 * g


def group_no(g):
    return g if g < LR_AT // 4 else g + 1


LR_GROUP = LR_AT // 4

C_COS, C_SIN, C_IDENT, C_BLOCK, C_KEEP, C_INVC, C_BSEL, C_END = 0, 320, 640, 768, 896, 1216, 1280, 1288
R_NG, R_QG, R_KG, R_SINK, R_SSINK, R_PS, R_BG, R_GG, R_END = 0, 16, 17, 18, 34, 35, 43, 47, 49


def side_steps():
    at = {}

    def put(beat, name, k, banks):
        at.setdefault(beat, []).append((name, k, banks))

    put(10, "gate", 0, (0, 1, 2, 3))
    for k in range(8):
        put(19 + 2 * k, "level", k, (0, 1, 2) if k <= 3 else (0, 1))
    for k in range(4):
        put(22 + 4 * k, "v_turn_prompt", k, (3,))
        put(23 + 4 * k, "v_turn_sample", k, (3,))
    put(37, "k_turn", 0, (0, 1, 2))
    for k in range(4):
        put(39 + 4 * k + k // 3, "pool", k, (2, 3))
    put(41, "first_chunk", 0, (0, 1, 2, 3))
    put(45, "second_chunk", 0, (0, 1, 2, 3))
    for k in range(8):
        put(53 + 2 * k, "sample_gla", k, (0, 1, 3))
    for k in range(2):
        put(69 + 2 * k, "gla_norm", k, (0, 1))
    put(72, "k_norm", 0, (2, 3))
    put(75, "kv_turn", 0, (2, 3))
    for k in range(4):
        put(79 + 4 * k, "q_norm", k, (2, 3))
    for j in range(8):
        n, banks = (82 + 4 * j, (0, 1)) if j < 3 else (93 + 2 * (j - 3), ((2, 3), (0, 1))[(j - 3) % 2])
        put(n, "scores", j, banks)
        put(n + 2, "p_turn", j, banks)
        put(n + 3, "pv", j, banks)
    for k in range(4):
        n = 103 + 2 * k
        put(n, "sample_scores", k, (k % 2,))
        put(n + 2, "sample_p_turn", k, (k % 2,))
        put(n + 3, "sample_pv", k, (2,))
    return at


STEPS = side_steps()
ORDER = [(n, k) for b in sorted(STEPS) for n, k, _ in STEPS[b]]
BANKS = {(n, k): banks for b in STEPS for n, k, banks in STEPS[b]}
STEP_NO = {s: i for i, s in enumerate(ORDER)}
N_STEPS = len(ORDER)
PROBS_AT = {}
for _b in sorted(STEPS):
    for _n, _k, _ in STEPS[_b]:
        if _n.endswith("p_turn"):
            PROBS_AT.setdefault(_b - 1, []).append((_n.replace("p_turn", "scores"), _k))
TAKE = {g: first_beat(g) + 3 for g in range(N_IN)}
TAKE.update({g: first_beat(g) + 4 for g in range(G_CZ, G_AZ + 1)})
TAKE.update({27: 115, 28: 118})
TAKEN_AT = {b: g for g, b in TAKE.items()}
GATED = [g for g in range(N_IN) if G_BZ <= g < G_K or g >= G_CZ]


def gated_at(beat, stage):
    wait = {G_AZ: 2}
    return [g for g in GATED if TAKE[g] + wait.get(g, 0) + stage == beat and g != GATED[-1]]


STACK_AT = (39, 40, 47, 48)


def state_load(l, k):
    per_layer = len(range(k % STATES, 8, STATES))
    return per_layer * l + k // STATES + 1


def slot_banks(j):
    return BANKS[("scores", j)]


def trunk(nc, ins, outs):
    with ExitStack() as ctx:
        def sem(name):
            return ctx.enter_context(nc.semaphore(name))

        top = [nc.sbuf_base + 64 - nc.sbuf_base % 64]

        def place(name, shape, dt=F32, at=None):
            size = {F32: 4, F32R: 4, BF16: 2, U8: 1}[dt]
            for s in shape[1:]:
                size *= s
            if at is None:
                at = top[0]
                top[0] += -(-size // 64) * 64
            return nc.alloc_sbuf_tensor_at(name, shape, dt, offset=at)

        xg_hi = place("xg_hi", [P, KT_D, TOK], F32R)
        xg_lo = place("xg_lo", [P, KT_D, TOK], F32R)
        mix0 = top[0]
        mg_hi = place("mg_hi", [P, KT_D, TOK], F32R)
        mg_lo = place("mg_lo", [P, KT_D, TOK], F32R)
        br0 = top[0]
        T1 = TOK * 4
        part_b, part_c, part_a = br0, br0 + 16 * T1, br0 + 32 * T1
        top[0] += 48 * T1
        br_hi = [None] * 3
        br_lo = [None] * 3
        for n, at in ((BR_B, part_b), (BR_C, part_c), (BR_A, part_a)):
            br_hi[n] = place(f"branch_hi{n}", [P, 8, TOK], F32R, at=at)
            br_lo[n] = place(f"branch_lo{n}", [P, 8, TOK], F32R, at=at + 8 * T1)
        raw = [place(f"raw{i}", [P, 1024]) for i in range(4)]
        w_hi = [place(f"w_hi{i}", [P, 512], F32R) for i in range(4)]
        w_lo = [place(f"w_lo{i}", [P, 512], F32R) for i in range(4)]
        const = place("const", [P, C_END])
        amask_p = place("amask_p", [P, 256], BF16)
        amask_s = place("amask_s", [P, 128 + NB * SMP], BF16)
        gmask = place("gmask", [P, 8, P], U8)
        par = place("par", [P, DEPTH, R_END])
        ones = place("ones", [P, P])
        eps = place("eps", [P, 1])
        rstd = place("rstd", [P, TOK])
        ta0 = top[0]
        ta = place("ta", [P, 2, TOK])
        tb = place("tb", [P, 2, TOK])
        tc = place("tc", [P, 2, TOK])
        att_s = place("att_s", [P, GH * SMP])
        smalls = [place(f"small{i}", [P, 32]) for i in range(2)]
        edge = place("edge", [P, GH, 2 + NB])
        q_s = place("q_s", [P, 2, NB, 2, 4, TS])
        att0 = top[0]
        att_p = place("att_p", [P, 2, 512])
        probs0 = place("probs0", [P, 768])
        probs1 = place("probs1", [P, 768], at=att0)
        sq_sum = place("sq_sum", [P, TOK], at=att0)
        x_first = place("x_first", [P, KT_D, TOK], at=mix0)
        gmask_f = place("gmask_f", [P, 8, P], at=mix0 + 16 * T1)
        o_c = place("o_c", [P, 8, TOK], at=mix0)
        o_ab = place("o_ab", [P, 8, TOK], at=mix0 + 8 * T1)
        q_a = place("q_a", [P, 8, TOK], at=mix0 + 16 * T1)
        hist = place("hist", [P, 8, (1 + NB) * HIST], at=mix0 + 16 * T1)
        lev_e = place("lev_e", [P, GH, TOK], at=mix0 + 24 * T1)
        lev_k = place("lev_k", [P, GH, TOK], at=mix0 + 28 * T1)
        s1 = place("s1", [P, GH, DV], at=mix0 + 24 * T1)
        k_a = place("k_a", [P, 2, TOK], at=mix0 + 28 * T1)
        v_tok = place("v_tok", [P, 3, KVH * HD], at=mix0 + 24 * T1)
        EXT = HIST + SEQ + NB * (HIST + TS)
        ext = place("ext", [P, 2, EXT], at=part_b)
        sums = place("sums", [P, 2, EXT], at=part_b + 3648)
        sums2 = place("sums2", [P, 2, EXT], at=ta0)
        diff = place("diff", [P, 2, TOK], at=part_b + 7296)
        w_pool = place("w_pool", [P, 8, 256], at=part_b + 7296 + 2560)
        v_gla = place("v_gla", [P, 3, 1024], at=part_c)
        ko_tok = place("ko_tok", [P, 3, GH * DK], at=part_c + 12288)
        k_sel = place("k_sel", [P, 4, DK], F32R, at=part_c + 12288 + 6144)
        k_stack = place("k_stack", [P, 2, GH * DK], F32R, at=mix0 + 28 * T1)
        v_stack = [place("v_stack0", [P, 1024], F32R), place("v_stack1", [P, 1024], F32R, at=att0)]
        squares = place("squares", [P, 4, TOK], at=part_c)
        w_gate = place("w_gate", [P, GH * DK], at=part_c + 12288 + 6144)
        cq = place("cq", [P, GH, TOK], at=part_a)
        ck = place("ck", [P, GH, TOK], at=part_a + 4 * T1)
        cb = place("cb", [P, GH, TOK], at=part_a + 8 * T1)
        lev_q = place("lev_q", [P, GH, TOK], at=part_a + 12 * T1)
        state = place("state", [P, STATES, 4, DV], at=part_a)
        cache_k = place("cache_k", [P, 2, NB, WINDOW], at=part_a)
        cache_v = place("cache_v", [P, NB, KVH * HD], at=part_a + 8192)
        probs = [probs0, probs1]

        main = ctx.enter_context(nc.psum_tensor("main", [P, 4, 512], F32))
        side = ctx.enter_context(nc.psum_tensor("side", [P, 4, 512], F32))
        rms_psum = side[:, 0, 0:TOK]

        raw_in = [sem(f"raw_in{i}") for i in range(4)]
        hi_ready = sem("hi_ready")
        lo_ready = sem("lo_ready")
        half_used = sem("half_used")
        main_free = sem("main_free")
        step_done = sem("step_done")
        vec_done = sem("vec_done")
        act_done = sem("act_done")
        act_given = sem("act_given")
        gate_sigmoid = sem("gate_sigmoid")
        gated_hi = sem("gated_hi")
        exps_done = sem("exps_done")
        stack_hi = sem("stack_hi")
        level_exp = sem("level_exp")
        level_k = sem("level_k")
        softplus_done = sem("softplus_done")
        swapped = sem("swapped")
        params_in = sem("params_in")
        rms_done = sem("rms_done")
        consts_in = sem("consts_in")
        x_in = [sem(f"x_in{j}") for j in range(8)]
        hist_in = sem("hist_in")
        w_pool_in = sem("w_pool_in")
        w_gate_in = sem("w_gate_in")
        state_in = [sem(f"state_in{i}") for i in range(STATES)]
        caches_in = sem("caches_in")
        res_in = [sem(f"res_in{i}") for i in range(2)]
        y_out = [sem(f"y_out{i}") for i in range(2)]
        state_out = [sem(f"state_out{i}") for i in range(STATES)]
        hist_out = sem("hist_out")
        kv_out = sem("kv_out")
        s2_out = sem("s2_out")
        window_out = sem("window_out")

        marks = {}

        def wait_mark(e, *key):
            s, v = marks[key]
            e.wait_ge(s, v)

        class Counted:

            def __init__(self, e, s):
                self.e, self.s, self.n, self.loop = e, s, 0, 0

            def value(self):
                return self.loop + self.n

            def __call__(self, instruction):
                instruction.then_inc(self.s, 1)
                self.n += 1

            def settle(self):
                self.e.wait_ge(self.s, self.value())

            def mark(self, *key):
                marks[key] = (self.s, self.value())

        def col(l, c, lo=0, hi=P):
            return par[lo:hi, l, c:c + 1]

        def two(t):
            return t.unsqueeze(1).to_broadcast([t.shape[0], 2, t.shape[1]])

        cosb = two(const[:, C_COS:C_COS + TOK])
        sinb = two(const[:, C_SIN:C_SIN + TOK])
        ident = const[:, C_IDENT:C_IDENT + P]
        head_ones = const[:, C_BLOCK:C_BLOCK + P]
        keep = const[:, C_KEEP:C_KEEP + TOK]

        def group_psum(G, n=2):
            b = 2 * (G % 2)
            return main[:, b:b + n, 0:TOK]

        def last_half(l, beat):
            return 2 * (BEATS * l + beat + 1)

        def segs(t3, B):
            n = TOK if B <= 4 else SEQ
            return t3[:, :, 0:n].rearrange("p h (a b) -> p h a b", b=2 * B), n // (2 * B)

        def odd_blocks(t3, B, lo=0, hi=None):
            t4 = t3[:, :, lo:hi].rearrange("p h (a b) -> p h a b", b=2 * B)
            return t4[:, :, :, B:2 * B]

        def even_blocks(t3, B, n):
            return t3[:, :, 0:n].rearrange("p h (a b) -> p h a b", b=2 * B)[:, :, :, 0:B]

        block = ctx.enter_context(nc.Block())

        @block.vector
        def _(dve):
            v = Counted(dve, vec_done)
            given = [0]

            def from_act():
                given[0] += 1
                dve.wait_ge(act_given, loop_given[0] + given[0])

            loop_given = [0]
            free = [0]

            def split_lo(Q, s0):
                for s in range(2):
                    i = (2 * s0 + s) % 4
                    dve.wait_ge(hi_ready, Q * 2 + (s + 1))
                    dve.tensor_tensor(w_lo[i][:, :], raw[s0 % 4][:, 512 * s:512 * s + 512],
                                      w_hi[i][:, :].bitcast(F32), ALU.subtract).then_inc(lo_ready, 1)

            def wait_step(l, name, k):
                dve.wait_ge(step_done, N_STEPS * l + STEP_NO[(name, k)] + 1)

            def read_group(l, G, beat_end, op):
                dve.wait_ge(half_used, beat_end)
                op(group_psum(G)).then_inc(main_free, 1)

            def settle_group(G):
                dve.wait_ge(main_free, G + 1)

            def tt(out, a, b, op):
                v(dve.tensor_tensor(out, a, b, op))
                v.settle()

            def stt(out, a, s, b, op0, op1):
                v(dve.scalar_tensor_tensor(out, a, s, b, op0, op1))
                v.settle()

            v(dve.memset(ones[:, :], 1.0))
            v(dve.memset(eps[:, :], EPS))
            v.settle()
            v.mark("start", 0, 0)
            dve.wait_ge(params_in, 16)

            def first_x(j):
                from_act()
                sq = (tb, tc)[j % 2]
                for t in range(2):
                    c = 2 * j + t
                    v(dve.scalar_tensor_tensor(xg_lo[:, c, :], x_first[:, c, :], col(0, R_NG + c),
                                               xg_hi[:, c, :].bitcast(F32), ALU.mult, ALU.subtract))
                v.mark("xg", 0, j)
                if j == 0:
                    v(dve.tensor_tensor(sq_sum[:, :], sq[:, 0, :], sq[:, 1, :], ALU.add))
                else:
                    for t in range(2):
                        v.settle()
                        v(dve.tensor_tensor(sq_sum[:, :], sq_sum[:, :], sq[:, t, :], ALU.add))
                v.mark("squares_added", 0, j)

            def take(l, g):
                G = GROUPS * l + group_no(g)
                end = last_half(l, first_beat(g) + 3)
                r2 = two(rstd[:, :])
                if g < G_CK:
                    read_group(l, G, end, lambda ps: dve.scalar_tensor_tensor(
                        cq[:, 2 * g:2 * g + 2, :], ps, float(DK) ** -0.5, r2, ALU.mult, ALU.mult))
                elif g < G_CV:
                    i = 2 * (g - G_CK)
                    read_group(l, G, end, lambda ps: dve.tensor_tensor(ck[:, i:i + 2, :], ps, r2, ALU.mult))
                elif g < G_U:
                    i = 2 * (g - G_CV)
                    read_group(l, G, end, lambda ps: dve.tensor_tensor(o_c[:, i:i + 2, :], ps, r2, ALU.mult))
                elif g < G_BZ:
                    pool_pair(l, g - G_U, G, end)
                elif g in (G_K, G_V) or G_Q <= g < G_CZ:
                    dst = ta if g != G_V else tb
                    if g == G_Q:
                        dve.wait_ge(kv_out, 48 * l + 48)
                    read_group(l, G, end, lambda ps: dve.tensor_tensor(dst[:, :, :], ps, r2, ALU.mult))
                else:
                    gate_pair(l, g, G, end)
                marks[("taken", l, g)] = (main_free, G + 1)
                if g < G_U or G_K <= g < G_CZ:
                    settle_group(G)

            pool_src = [None]

            def pool_pair(l, gi, G, end):
                w = 2 << gi
                dve.wait_ge(half_used, end)
                from_act()
                if gi:
                    wait_step(l, "pool", gi - 1)
                ps = group_psum(G)
                for t in range(2):
                    x = ext[:, t, :]
                    v(dve.tensor_tensor(x[:, HIST:HIST + SEQ], ps[:, t, 0:SEQ], rstd[:, 0:SEQ], ALU.mult))
                    out = x[:, HIST + SEQ:EXT].rearrange("p (b t) -> p b t", t=HIST + TS)[:, :, HIST:]
                    last = dve.tensor_tensor(out, ps[:, t, SEQ:TOK].rearrange("p (b t) -> p b t", t=TS),
                                             rstd[:, SEQ:TOK].rearrange("p (b t) -> p b t", t=TS), ALU.mult)
                    if t == 0:
                        v(last)
                last.then_inc(main_free, 1)
                settle_group(G)
                marks[("ext_full", l, gi)] = (main_free, G + 1)
                src, step = ext, 1
                for i in range(gi + 1):
                    n = 2 * step - 1
                    dst = (sums, sums2)[i % 2]
                    tt(dst[:, :, n:EXT], src[:, :, n:EXT], src[:, :, n - step:EXT - step], ALU.add)
                    src, step = dst, 2 * step
                pool_src[0] = src

            def pool_diff(l, gi):
                w, src = 2 << gi, pool_src[0]
                stt(diff[:, :, 0:SEQ], src[:, :, HIST:HIST + SEQ], 1.0 / w, ext[:, :, HIST:HIST + SEQ],
                    ALU.mult, ALU.subtract)
                inv = two(const[:, C_INVC + 16 * gi:C_INVC + 16 * gi + 16])
                tt(tc[:, :, 0:16], src[:, :, HIST:HIST + 16], inv, ALU.mult)
                tt(diff[:, :, 0:16], tc[:, :, 0:16], ext[:, :, HIST:HIST + 16], ALU.subtract)
                for t in range(2):
                    def smp(z):
                        return z[:, t, HIST + SEQ:EXT].rearrange("p (b t) -> p b t", t=HIST + TS)[:, :, HIST:]
                    v(dve.scalar_tensor_tensor(diff[:, t, SEQ:TOK].rearrange("p (b t) -> p b t", t=TS), smp(src),
                                               1.0 / w, smp(ext), ALU.mult, ALU.subtract))
                v.settle()
                v.mark("diff", l, gi)

            def gated_parts(g):
                n, g0, o = ((BR_B, G_BZ, o_ab) if g < G_K else (BR_C, G_CZ, o_c) if g < G_AZ else (BR_A, G_AZ, o_ab))
                return n, o, 2 * (g - g0)

            def gate_pair(l, g, G, end):
                if g == G_BZ:
                    dve.wait_ge(hist_out, 16 * l + 16)
                read_group(l, G, end, lambda ps: dve.tensor_tensor(ta[:, :, :], ps, two(rstd[:, :]), ALU.mult))
                settle_group(G)

            def gate_product(l, g):
                n, o, i = gated_parts(g)
                if g == G_AZ:
                    from_act()
                dve.wait_ge(gate_sigmoid, len(GATED) * l + GATED.index(g) + 1)
                tt(ta[:, :, :], ta[:, :, :], tc[:, :, :], ALU.mult)
                tt(ta[:, :, :], ta[:, :, :], o[:, i:i + 2, :], ALU.mult)
                v.mark("gated", l, g)

            def gate_low(l, g):
                n, o, i = gated_parts(g)
                dve.wait_ge(gated_hi, len(GATED) * l + GATED.index(g) + 1)
                v(dve.tensor_tensor(br_lo[n][:, i:i + 2, :], ta[:, :, :], br_hi[n][:, i:i + 2, :].bitcast(F32),
                                    ALU.subtract))
                v.settle()
                v.mark("branch", l, g)

            def log_decay(l):
                wait_step(l, "gate", 0)
                for h in range(GH):
                    v(dve.tensor_scalar(lev_q[:, h, :], side[:, h, 0:TOK], col(l, R_BG + h), None, ALU.add))
                v.settle()
                v.mark("gate_in", l, 0)

            def log_decay_sum(l):
                dve.wait_ge(softplus_done, l + 1)
                v(dve.tensor_scalar(lev_q[:, :, :], lev_q[:, :, :], 0.0, 1.0 / 16.0, ALU.min, ALU.mult))
                v.settle()
                stt(lev_q[:, :, :], lev_e[:, :, :], -1.0 / 16.0, lev_q[:, :, :], ALU.mult, ALU.add)
                for h in range(GH):
                    v(dve.tensor_tensor_scan(cb[:, h, :], keep, lev_q[:, h, :], 0.0, ALU.mult, ALU.add))
                v.settle()
                v(dve.memset(att_p[:, :, :], 0.0))
                v(dve.memset(att_s[:, :], 0.0))
                v.settle()
                v.mark("decay", l, 0)

            def level_prep(l, k):
                B = LEVELS[k - 1]
                e4, n = segs(lev_e, B)
                b4, _ = segs(cb, B)
                if k > 1:
                    dve.wait_ge(level_k, 7 * l + k - 1)
                v(dve.tensor_tensor(e4, b4, b4[:, :, :, B - 1:B].to_broadcast([P, GH, n, 2 * B]), ALU.subtract))
                v.mark("level_gap", l, k)

            def level_scale(l, k):
                B = LEVELS[k - 1]
                w = segs(lev_e, B)[1] * 2 * B
                dve.wait_ge(level_exp, 7 * l + k)
                v(dve.tensor_tensor(odd_blocks(lev_q, B, 0, w), odd_blocks(cq, B, 0, w), odd_blocks(lev_e, B, 0, w), ALU.mult))
                v.mark("level", l, k)

            def level_take(l, k):
                wait_step(l, "level", k)
                B = LEVELS[k - 1] if k else 0
                for c in range(3 if k <= 3 else 2):
                    rows, n = (P, P) if c < 2 else (SMP, SMP)
                    att = (att_p[:, c, :] if c < 2 else att_s[0:SMP, :]).rearrange("p (h t) -> p h t", h=GH)
                    mask = gmask[0:rows, k:k + 1, 0:n]
                    got = side[0:rows, c, 0:GH * (n // 2 if k else n)].rearrange("p (h t) -> p h t", h=GH)
                    if k:
                        att, mask = odd_blocks(att, B), odd_blocks(mask, B)
                        got = got.rearrange("p h (a b) -> p h a b", b=B)
                    mask = mask.to_broadcast([rows, GH] + list(att.shape[2:]))
                    if B == 1:
                        att, mask, got = (z.rearrange("p h a b -> p h (a b)") for z in (att, mask, got))
                    v(dve.copy_predicated(att, mask, got))
                v.settle()
                v.mark("att", l, k)

            def carry_prep(l):
                wait_step(l, "level", 7)
                dve.wait_ge(level_k, 7 * l + 7)
                from_act()
                tt(lev_q[:, :, :], cq[:, :, :], lev_e[:, :, :], ALU.mult)
                for h in range(GH):
                    for lo, hi, n in ((0, SEQ, P), (SEQ, TOK, TS)):
                        b3 = cb[:, h, lo:hi].rearrange("p (a b) -> p a b", b=n)
                        v(dve.tensor_tensor(lev_e[:, h, lo:hi].rearrange("p (a b) -> p a b", b=n),
                                            b3[:, :, n - 1:n].to_broadcast([P, (hi - lo) // n, n]), b3, ALU.subtract))
                v.settle()
                v.mark("end_gap", l, 0)

            def carry_end(l):
                from_act()
                v(dve.tensor_tensor(lev_k[:, :, :], ck[:, :, :], lev_e[:, :, :], ALU.mult))
                v.settle()
                v.mark("carry", l, 0)

            def second_state(l):
                wait_step(l, "second_chunk", 0)
                for h in range(GH):
                    v(dve.scalar_tensor_tensor(s1[:, h, :], s1[:, h, :], edge[:, h, 1:2],
                                               side[:, 2 + h // 2, 256 * (h % 2):256 * (h % 2) + 256],
                                               ALU.mult, ALU.add))
                v.settle()
                v.mark("second_state", l, 0)

            def sample_sel(l, k):
                h, half = divmod(k, 2)
                if k:
                    wait_step(l, "sample_gla", k - 1)
                src = k_stack[0:96, half, DK * h:DK * h + DK].bitcast(F32).unsqueeze(1).to_broadcast([96, 4, DK])
                sel = const[0:96, C_BSEL:C_BSEL + 4].unsqueeze(2).to_broadcast([96, 4, DK])
                v(dve.tensor_tensor(k_sel[0:96, :, :], src, sel, ALU.mult))
                v.mark("k_sel", l, k)

            def stack_low(l, n):
                half = n % 2
                rows = slice(32 * half, 32 * half + 32)
                dve.wait_ge(stack_hi, 4 * l + n + 1)
                if n < 2:
                    v(dve.tensor_tensor(k_stack[64:96, half, :], ko_tok[rows, 2, :],
                                        k_stack[rows, half, :].bitcast(F32), ALU.subtract))
                else:
                    out = slice(32 * (1 - half), 32 * (1 - half) + 32)
                    v(dve.tensor_tensor(v_stack[half][out, :], v_gla[rows, 2, :],
                                        v_stack[half][rows, :].bitcast(F32), ALU.subtract))
                v.settle()
                v.mark("stack", l, n)

            def sample_state(l, k):
                h, half = divmod(k, 2)
                wait_step(l, "sample_gla", k)
                for b in range(4):
                    v(dve.scalar_tensor_tensor(state[:, k % STATES, b, :], state[:, k % STATES, b, :],
                                               edge[:, h, 2 + 4 * half + b:3 + 4 * half + b],
                                               side[:, b // 2, 256 * (b % 2):256 * (b % 2) + 256],
                                               ALU.mult, ALU.add))
                v.settle()
                v.mark("sample_state", l, k)

            def gla_scale(l, k):
                from_act()
                for i in range(2):
                    for t in range(2):
                        c = 4 * k + 2 * i + t
                        v(dve.scalar_tensor_tensor(o_c[:, c, :], o_c[:, c, :], col(l, R_GG + t), tb[:, i, :],
                                                   ALU.mult, ALU.mult))
                v.settle()
                v.mark("gla_scaled", l, k)

            def rope_pair(l, name, k):
                out, g = (k_a[:, :, :], R_KG) if name == "k_norm" else (q_a[:, 2 * k:2 * k + 2, :], R_QG)
                from_act()
                stt(ta[:, :, :], ta[:, :, :], col(l, g), tb[:, :, :], ALU.mult, ALU.mult)
                v.mark("normed", l, (name, k))
                v(dve.tensor_tensor(out, ta[:, :, :], cosb, ALU.mult))

            def rope_end(l, name, k):
                out = k_a[:, :, :] if name == "k_norm" else q_a[:, 2 * k:2 * k + 2, :]
                dve.wait_ge(swapped, 5 * l + (1 if name == "k_norm" else 2 + k))
                tt(tc[:, :, :], tc[:, :, :], sinb, ALU.mult)
                tt(out, out, tc[:, :, :], ALU.add)
                if name == "q_norm":
                    for t in range(2):
                        for i in range(2):
                            rows = slice(HD * i, HD * i + HD)
                            v(dve.tensor_copy(q_s[rows, k // 2, :, i, 2 * (k % 2) + t, :],
                                              q_a[rows, 2 * k + t, SEQ:TOK].rearrange("p (b t) -> p b t", t=TS)))
                    v.settle()
                v.mark("roped", l, (name, k))

            def prompt_softmax(l, j):
                p, small = probs[j % 2], smalls[j % 2]
                b0, b1 = slot_banks(j)
                wait_step(l, "scores", j)
                p2 = p[:, :].rearrange("p (h k) -> p h k", h=2)
                late = p2[:, :, 0:256]
                early = p2[:, :, 256:384]
                v(dve.scalar_tensor_tensor(late, side[:, b0:b0 + 2, 0:256], HD ** -0.5, two(amask_p[:, :]),
                                           ALU.mult, ALU.add))
                v(dve.scalar_tensor_tensor(early, side[:, b0:b0 + 2, 256:384], HD ** -0.5, two(amask_p[:, 128:256]),
                                           ALU.mult, ALU.add))
                v.settle()
                v(dve.tensor_reduce(small[:, 0:2], late, AX.X, ALU.max))
                v(dve.tensor_reduce(small[:, 2:4], early, AX.X, ALU.max))
                v.settle()
                sink = par[:, l, R_SINK + 2 * j:R_SINK + 2 * j + 2]
                for i in (0, 2):
                    v(dve.tensor_tensor(small[:, i:i + 2], small[:, i:i + 2], sink, ALU.max))
                v.settle()
                v(dve.tensor_scalar(small[:, 4:8], small[:, 0:4], -1.0, None, ALU.mult))
                for i in (0, 2):
                    v(dve.tensor_tensor(small[:, 8 + i:10 + i], sink, small[:, i:i + 2], ALU.subtract))
                v.settle()
                v.mark("masked", l, j)

            def prompt_probs(l, j):
                p, small = probs[j % 2], smalls[j % 2]
                p2 = p[:, :].rearrange("p (h k) -> p h k", h=2)
                late, early = p2[:, :, 0:256], p2[:, :, 256:384]
                dve.wait_ge(exps_done, 12 * l + j + 1)
                tt(small[:, 16:20], small[:, 12:16], small[:, 20:24], ALU.add)
                v(dve.reciprocal(small[:, 16:20], small[:, 16:20]))
                v.settle()
                for i in range(2):
                    v(dve.tensor_scalar(late[:, i], late[:, i], small[:, 16 + i:17 + i], None, ALU.mult))
                    v(dve.tensor_scalar(early[:, i], early[:, i], small[:, 18 + i:19 + i], None, ALU.mult))
                v.settle()
                v.mark("probs", l, j)

            def sample_softmax(l, k):
                p, small = probs[k % 2], smalls[k % 2]
                b0, = BANKS[("sample_scores", k)]
                wait_step(l, "sample_scores", k)
                s3 = side[:, b0, 0:384].rearrange("p (b k) -> p b k", b=2)
                p3 = p[:, 0:384].rearrange("p (b k) -> p b k", b=2)
                new = amask_s[:, 128 + 2 * k * SMP:128 + 2 * (k + 1) * SMP].rearrange("p (b k) -> p b k", b=2)
                v(dve.scalar_tensor_tensor(p3[:, :, 0:128], s3[:, :, 0:128], HD ** -0.5, two(amask_s[:, 0:128]),
                                           ALU.mult, ALU.add))
                v(dve.scalar_tensor_tensor(p3[:, :, 128:192], s3[:, :, 128:192], HD ** -0.5, new, ALU.mult, ALU.add))
                v.settle()
                v(dve.tensor_reduce(small[:, 0:2], p3, AX.X, ALU.max))
                v.settle()
                v(dve.tensor_scalar(small[:, 0:2], small[:, 0:2], col(l, R_SSINK), None, ALU.max))
                v.settle()
                v(dve.tensor_scalar(small[:, 4:6], small[:, 0:2], -1.0, None, ALU.mult))
                v.settle()
                v(dve.tensor_scalar(small[:, 8:10], small[:, 4:6], col(l, R_SSINK), None, ALU.add))
                v.settle()
                v.mark("sample_masked", l, k)

            def sample_probs(l, k):
                small = smalls[k % 2]
                p3 = probs[k % 2][:, 0:384].rearrange("p (b k) -> p b k", b=2)
                dve.wait_ge(exps_done, 12 * l + 8 + k + 1)
                tt(small[:, 16:18], small[:, 12:14], small[:, 20:22], ALU.add)
                v(dve.reciprocal(small[:, 16:18], small[:, 16:18]))
                v.settle()
                for i in range(2):
                    v(dve.tensor_scalar(p3[:, i], p3[:, i], small[:, 16 + i:17 + i], None, ALU.mult))
                v.settle()
                v.mark("sample_probs", l, k)

            def vector_part(l, beat):
                if l == 0 and beat < 2:
                    for j in range(4 + 2 * beat, 6 + 2 * beat):
                        first_x(j)
                if l == 0 and beat == 1:
                    v.settle()
                    v.mark("sq_sum", 0, 0)
                if l == 0 and beat == 5:
                    dve.wait_ge(consts_in, 64)
                    v(dve.tensor_copy(gmask[:, :, :], gmask_f[:, :, :]))
                    v(dve.memset(q_s[:, :, :, :, :, :].rearrange("p i b j g t -> p (i b j g t)"), 0.0))
                    v.mark("masks", 0, 0)
                if beat == 3:
                    from_act()
                if beat == LR_AT + 1:
                    for i in range(2 if l else 0):
                        dve.wait_ge(y_out[i], 64 * l)
                    dve.wait_ge(half_used, last_half(l, beat))
                    dve.tensor_tensor(ta[:, 0, :], group_psum(GROUPS * l + LR_GROUP)[:, 0, :], rstd[:, :],
                                      ALU.mult).then_inc(main_free, 1)
                    marks[("lr", l, 0)] = (main_free, GROUPS * l + LR_GROUP + 1)
                if beat == 12:
                    log_decay_sum(l)
                if beat == 14:
                    v(dve.memset(lev_k[:, :, :], 0.0))
                    v.mark("keys_clear", l, 0)
                for name, k in PROBS_AT.get(beat, ()):
                    if name == "scores":
                        prompt_probs(l, k)
                    elif name == "sample_scores":
                        sample_probs(l, k)
                for g in gated_at(beat, 2):
                    gate_low(l, g)
                for g in gated_at(beat, 1):
                    gate_product(l, g)
                for name, k, _ in STEPS.get(beat - 2, ()):
                    if name in ("k_norm", "q_norm"):
                        rope_end(l, name, k)
                if TAKEN_AT.get(beat, G_CZ) < G_CZ:
                    take(l, TAKEN_AT[beat])
                for gi in range(4):
                    if beat == TAKE[G_U + gi] + 1:
                        pool_diff(l, gi)
                for k in range(8):
                    if k and beat == 18 + 2 * k:
                        level_scale(l, k)
                for name, k, _ in STEPS.get(beat, ()):
                    if name == "gate":
                        log_decay(l)
                    elif name == "level":
                        level_take(l, k)
                    elif name == "pool":
                        wait_step(l, "pool", k)
                        for t in range(2):
                            v(dve.tensor_scalar(o_ab[:, 2 * k + t, :], side[:, 2 + t, 0:TOK],
                                                col(l, R_PS + 2 * k + t), None, ALU.mult))
                        v.settle()
                        v.mark("pooled", l, k)
                    elif name == "second_chunk":
                        second_state(l)
                    elif name == "sample_gla":
                        sample_state(l, k)
                    elif name == "gla_norm":
                        gla_scale(l, k)
                    elif name in ("k_norm", "q_norm"):
                        rope_pair(l, name, k)
                    elif name == "scores":
                        prompt_softmax(l, k)
                    elif name == "sample_scores":
                        sample_softmax(l, k)
                if TAKEN_AT.get(beat, 0) >= G_CZ:
                    take(l, TAKEN_AT[beat])
                if beat == TAKE[GATED[-1]]:
                    gate_product(l, GATED[-1])
                    gate_low(l, GATED[-1])
                for k in range(1, 8):
                    if beat == 17 + 2 * k:
                        level_prep(l, k)
                if beat == 34:
                    carry_prep(l)
                if beat == 36:
                    carry_end(l)
                if beat in STACK_AT:
                    stack_low(l, STACK_AT.index(beat))
                for k in range(8):
                    if beat == 51 + 2 * k:
                        sample_sel(l, k)
                if beat in (68, 70):
                    from_act()
                    v(dve.tensor_tensor(squares[:, 0:4:2, :], squares[:, 0:4:2, :], squares[:, 1:4:2, :], ALU.add))
                    v.mark("squares", l, (beat - 68) // 2)

            def mix_body(l, i, py):
                Q0 = BEATS * l + IN_BEATS
                G0 = GROUPS * l + 1 + N_IN
                b = 0
                for jj in range(2):
                    for n in range(3):
                        for part in range(6):
                            split_lo(i * 36 + (Q0 + b + 2), Q0 + b + 2)
                            b += 1
                            if part == 3:
                                dve.wait_ge(half_used, i * 72 + 2 * (Q0 + b))
                                dve.tensor_tensor(ta[:, :, :], group_psum(G0), two(rstd[:, :]),
                                                  ALU.mult).then_inc(main_free, 1)
                        dve.wait_ge(half_used, i * 72 + 2 * (Q0 + b))
                        from_act()
                        dst = tc if n == 0 else ta
                        v.settle()
                        dve.tensor_tensor(dst[:, :, :], group_psum(G0 + 1), tb[:, :, :],
                                          ALU.mult).then_inc(main_free, 1)
                        dve.wait_ge(main_free, i * 12 + (G0 + 6 * jj + 2 * n + 2))
                        if n:
                            tt(tc[:, :, :], tc[:, :, :], ta[:, :, :], ALU.add)
                    at = i * 4 + 2 * jj
                    hi = mg_hi[:, bass.ds(at, 2), :] if not py else mg_hi[:, at:at + 2, :]
                    lo = mg_lo[:, bass.ds(at, 2), :] if not py else mg_lo[:, at:at + 2, :]
                    v(dve.tensor_scalar(hi, tc[:, :, :], 1.0, None, ALU.mult))
                    v.settle()
                    v(dve.tensor_tensor(lo, tc[:, :, :], hi.bitcast(F32), ALU.subtract))

            def out_body(l, i, py, last_layer):
                Q0 = BEATS * l + IN_BEATS + MIX_BEATS
                G0 = GROUPS * l + 1 + N_IN + 6 * PAIRS
                for jj in range(2):
                    for part in range(4):
                        b = 4 * jj + part
                        if not (last_layer and py and b >= 6):
                            split_lo(i * 8 + (Q0 + b + 2), Q0 + b + 2)
                    y = (ta, tb)[jj]
                    dve.wait_ge(res_in[jj], i * 16 + (64 * l + 16))
                    dve.wait_ge(half_used, i * 16 + 2 * (Q0 + 4 * jj + 4))
                    dve.tensor_tensor(y[:, :, :], y[:, :, :], group_psum(G0 + jj), ALU.add).then_inc(main_free, 1)
                    dve.wait_ge(main_free, i * 2 + (G0 + jj + 1))
                    if not last_layer:
                        for t in range(2):
                            at = i * 4 + (2 * jj + t)
                            g = par[:, l + 1, R_NG:R_NG + KT_D][:, bass.ds(at, 1)]
                            hi = xg_hi[:, bass.ds(at, 1), :].rearrange("p a t -> p (a t)")
                            lo = xg_lo[:, bass.ds(at, 1), :].rearrange("p a t -> p (a t)")
                            v(dve.tensor_scalar(hi, y[:, t, :], g, None, ALU.mult))
                            v.settle()
                            v(dve.scalar_tensor_tensor(lo, y[:, t, :], g, hi.bitcast(F32), ALU.mult, ALU.subtract))
                            v(dve.tensor_tensor(tc[:, t, :], y[:, t, :], y[:, t, :], ALU.mult))
                            v.settle()
                            v(dve.tensor_tensor(sq_sum[:, :], sq_sum[:, :], tc[:, t, :], ALU.add))

            for l in range(DEPTH):
                last_layer = l == DEPTH - 1
                for beat in range(IN_BEATS):
                    Q = BEATS * l + beat
                    if l == 0 and beat == 0:
                        first_x(0)
                        first_x(1)
                        split_lo(0, 0)
                        first_x(2)
                        first_x(3)
                        split_lo(1, 1)
                    split_lo(Q + 2, Q + 2)
                    vector_part(l, beat)
                v.mark("branches", l, 0)
                v.settle()
                base_v, base_g = v.n, given[0]
                per_v, per_g = 2 * (2 + 2), 6
                with dve.Fori(0, 4) as i:
                    v.loop, loop_given[0] = i * per_v, i * per_g
                    mix_body(l, i, False)
                assert v.n - base_v == per_v and given[0] - base_g == per_g, (v.n - base_v, given[0] - base_g)
                v.loop, loop_given[0] = 0, 0
                v.n, given[0] = base_v + 4 * per_v, base_g + 4 * per_g
                v.settle()
                v.mark("merged", l, 0)
                marks[("merged_first", l, 0)] = (vec_done, base_v + 3 * per_v)
                if not last_layer:
                    v(dve.memset(sq_sum[:, :], 0.0))
                    v.settle()
                    base_v = v.n
                    per_v = 16
                    with dve.Fori(0, 4) as i:
                        v.loop = i * per_v
                        out_body(l, i, False, False)
                    assert v.n - base_v == per_v
                    v.loop, v.n = 0, base_v + 4 * per_v
                    for j in range(8):
                        marks[("xg", l + 1, j)] = (vec_done, base_v + 8 * j + 8)
                    v.settle()
                    v.mark("sq_sum", l + 1, 0)
                else:
                    with dve.Fori(0, 3) as i:
                        out_body(l, i, False, True)
                    out_body(l, 3, True, True)

        @block.scalar
        def _(act):
            a = Counted(act, act_done)

            def give(instruction):
                instruction.then_inc(act_given, 1)
                given[0] += 1

            given = [0]
            table = [None]

            def use_ln_exp():
                if table[0] != LN_EXP_TABLE:
                    act.add_instruction(mybir.InstLoadActFuncSet(name=nc.get_next_instruction_name(),
                                                                 act_func_set_id=LN_EXP_TABLE))
                    table[0] = LN_EXP_TABLE

            def split_hi(Q, s0):
                act.wait_ge(raw_in[s0 % 4], (Q - s0) * 4 + (16 * (s0 // 4) + 16))
                for s in range(2):
                    i = (2 * s0 + s) % 4
                    if 2 * s0 + s >= 4:
                        act.wait_ge(half_used, Q * 2 + (s - 3))
                    act.activation(w_hi[i][:, :], raw[s0 % 4][:, 512 * s:512 * s + 512], ACT.Copy).then_inc(hi_ready, 1)

            def wait_step(l, name, k):
                act.wait_ge(step_done, N_STEPS * l + STEP_NO[(name, k)] + 1)

            def vec(*key):
                wait_mark(act, *key)

            act.dma_start(par[:, :, :], ins["params"]).then_inc(params_in, 16)
            for j in range(8):
                act.dma_start(x_first[:, 2 * j:2 * j + 2, :], ins["x_pairs"][j]).then_inc(x_in[j], 16)
            vec("start", 0, 0)
            act.wait_ge(params_in, 16)

            def inverse_root(out, ms, scale):
                use_ln_exp()
                a(act.activation(out, ms, ACT.Ln, scale=scale, bias=eps[:, :]))
                a.settle()
                give(act.activation(out, out, ACT.Exp, scale=-0.5))
                return act_done, a.value()

            def first_x(j):
                act.wait_ge(x_in[j], 16)
                for t in range(2):
                    c = 2 * j + t
                    a(act.activation(xg_hi[:, c, :], x_first[:, c, :], ACT.Copy, scale=col(0, R_NG + c)))
                if j >= 2:
                    vec("squares_added", 0, j - 2)
                give(act.activation((tb, tc)[j % 2][:, :, :], x_first[:, 2 * j:2 * j + 2, :], ACT.Square))

            def ext_fill(l, gi):
                if gi == 0:
                    act.wait_ge(hist_in, 16 * l + 16)
                else:
                    vec("diff", l, gi - 1)
                    a.settle()
                for t in range(2):
                    a(act.activation(ext[:, t, 0:HIST], hist[:, 2 * gi + t, 0:HIST], ACT.Copy))
                    last = act.activation(
                        ext[:, t, HIST + SEQ:EXT].rearrange("p (b t) -> p b t", t=HIST + TS)[:, :, 0:HIST],
                        hist[:, 2 * gi + t, HIST:].rearrange("p (b t) -> p b t", t=HIST), ACT.Copy)
                    if t == 0:
                        a(last)
                give(last)

            def hist_take(l, gi):
                vec("ext_full", l, gi)
                act.wait_ge(act_given, given[0])
                for t in range(2):
                    a(act.activation(hist[:, 2 * gi + t, 0:HIST], ext[:, t, SEQ:SEQ + HIST], ACT.Copy))
                    a(act.activation(
                        hist[:, 2 * gi + t, HIST:].rearrange("p (b t) -> p b t", t=HIST),
                        ext[:, t, HIST + SEQ:EXT].rearrange("p (b t) -> p b t", t=HIST + TS)[:, :, TS:], ACT.Copy))
                a.mark("hist", l, gi)

            def gate_high(l, g):
                n, g0 = (BR_B, G_BZ) if g < G_K else (BR_C, G_CZ) if g < G_AZ else (BR_A, G_AZ)
                i = 2 * (g - g0)
                vec("gated", l, g)
                act.activation(br_hi[n][:, i:i + 2, :], ta[:, :, :], ACT.Copy).then_inc(gated_hi, 1)

            def gate_take(l, g):
                if G_U <= g < G_BZ:
                    hist_take(l, g - G_U)
                if g in GATED:
                    if g == G_CZ:
                        vec("roped", l, ("q_norm", 3))
                    vec("taken", l, g)
                    act.activation(tc[:, :, :], ta[:, :, :], ACT.Sigmoid).then_inc(gate_sigmoid, 1)
                    table[0] = None
                if g == GATED[-1]:
                    gate_high(l, g)

            def scalar_part(l, beat):
                if l == 0 and beat < 2:
                    for j in range(4 + 2 * beat, 6 + 2 * beat):
                        first_x(j)
                if beat == 3:
                    act.wait_ge(rms_done, l + 1)
                    marks[("rms_taken", l, 0)] = inverse_root(rstd[:, :], rms_psum, 1.0 / D)
                if beat == 35:
                    vec("end_gap", l, 0)
                    give(act.activation(lev_e[:, :, :], lev_e[:, :, :], ACT.Exp))
                if beat in (35, 38, 42, 46):
                    ext_fill(l, {35: 0, 38: 1, 42: 2, 46: 3}[beat])
                if TAKEN_AT.get(beat, G_CZ) < G_CZ:
                    gate_take(l, TAKEN_AT[beat])
                for name, k, banks in STEPS.get(beat, ()):
                    if name == "gate":
                        use_ln_exp()
                        vec("gate_in", l, 0)
                        a(act.activation(lev_e[:, :, :], lev_q[:, :, :], ACT.Abs))
                        a.settle()
                        a(act.activation(lev_e[:, :, :], lev_e[:, :, :], ACT.Exp, scale=-1.0))
                        a.settle()
                        act.activation(lev_e[:, :, :], lev_e[:, :, :], ACT.Ln, bias=1.0).then_inc(softplus_done, 1)
                    elif name == "v_turn_prompt":
                        wait_step(l, name, k)
                        a(act.activation(v_gla[:, 0:2, 256 * k:256 * k + 256],
                                         side[:, 3, :].rearrange("p (c n) -> p c n", c=2), ACT.Copy))
                        a.mark(name, l, k)
                    elif name == "v_turn_sample":
                        wait_step(l, name, k)
                        a(act.activation(v_gla[0:SMP, 2, 256 * k:256 * k + 256], side[0:SMP, 3, 0:256], ACT.Copy))
                        a.mark(name, l, k)
                    elif name == "k_turn":
                        wait_step(l, name, k)
                        for c in range(2):
                            a(act.activation(ko_tok[:, c, :], side[:, c, :], ACT.Copy))
                        a(act.activation(ko_tok[0:SMP, 2, :], side[0:SMP, 2, :], ACT.Copy))
                        a.settle()
                        a.mark(name, l, k)
                    elif name == "first_chunk":
                        wait_step(l, name, k)
                        a(act.activation(s1[:, :, :], side[:, 0:2, :].rearrange("p b (h n) -> p (b h) n", h=2), ACT.Copy))
                        a(act.activation(o_c[:, :, 0:P], side[:, 2:4, :].rearrange("p b (c n) -> p (b c) n", c=4),
                                         ACT.Copy))
                        a.mark(name, l, k)
                    elif name == "second_chunk":
                        wait_step(l, name, k)
                        a(act.activation(o_c[:, :, P:SEQ], side[:, 0:2, :].rearrange("p b (c n) -> p (b c) n", c=4),
                                         ACT.Copy))
                        a.mark(name, l, k)
                    elif name == "sample_gla" and k == 7:
                        wait_step(l, name, k)
                        a(act.activation(o_c[:, :, SEQ:TOK], side[:, 3, :].rearrange("p (c n) -> p c n", c=8), ACT.Copy))
                        a.settle()
                        a.mark(name, l, k)
                    elif name == "gla_norm":
                        wait_step(l, name, k)
                        if k:
                            vec("gla_scaled", l, 0)
                        marks[("gla_ms", l, k)] = inverse_root(tb[:, :, :], side[:, 0:2, 0:TOK], 1.0 / DV)
                    elif name in ("k_norm", "q_norm"):
                        wait_step(l, name, k)
                        if name == "k_norm":
                            vec("gla_scaled", l, 1)
                        marks[("head_ms", l, (name, k))] = inverse_root(tb[:, :, :], side[:, 2:4, 0:TOK], 1.0 / HD)
                    elif name == "kv_turn":
                        wait_step(l, name, k)
                        act.wait_ge(s2_out, 16 * l + 16)
                        a(act.activation(v_tok[:, 0:2, :], side[:, 2, :].rearrange("p (c n) -> p c n", c=2), ACT.Copy))
                        a(act.activation(v_tok[0:SMP, 2, :], side[0:SMP, 3, 0:256], ACT.Copy))
                        a.mark(name, l, k)
                    elif name == "scores":
                        p, small = probs[k % 2], smalls[k % 2]
                        use_ln_exp()
                        vec("masked", l, k)
                        for i in range(4):
                            lo, n = ((0, 256), (384, 256), (256, 128), (640, 128))[i]
                            a(act.activation(p[:, lo:lo + n], p[:, lo:lo + n], ACT.Exp, bias=small[:, 4 + i:5 + i],
                                             accum_out=small[:, 12 + i:13 + i]))
                        act.activation(small[:, 20:24], small[:, 8:12], ACT.Exp).then_inc(exps_done, 1)
                    elif name == "p_turn":
                        wait_step(l, name, k)
                        a(act.activation(probs[k % 2][:, :].rearrange("p (h k) -> p h k", h=2),
                                         side[:, banks[0]:banks[0] + 2, 0:384], ACT.Copy))
                        a.mark(name, l, k)
                    elif name == "pv":
                        wait_step(l, name, k)
                        a(act.activation(o_ab[:, k, 0:SEQ].rearrange("p (c t) -> p c t", c=2),
                                         side[:, banks[0]:banks[0] + 2, 384:512], ACT.Copy))
                        a.mark(name, l, k)
                    elif name == "sample_scores":
                        p, small = probs[k % 2], smalls[k % 2]
                        use_ln_exp()
                        vec("sample_masked", l, k)
                        for i in range(2):
                            a(act.activation(p[:, 192 * i:192 * i + 192], p[:, 192 * i:192 * i + 192], ACT.Exp,
                                             bias=small[:, 4 + i:5 + i], accum_out=small[:, 12 + i:13 + i]))
                        act.activation(small[:, 20:22], small[:, 8:10], ACT.Exp).then_inc(exps_done, 1)
                    elif name == "sample_p_turn":
                        wait_step(l, name, k)
                        s3 = side[:, banks[0], :].rearrange("p (b n) -> p b n", b=4)
                        p3 = probs[k % 2][:, 0:512].rearrange("p (b n) -> p b n", b=4)
                        a(act.activation(p3[:, 0:2, :], s3[:, 0:2, :], ACT.Copy))
                        a(act.activation(p3[0:SMP, 2:4, :], s3[0:SMP, 2:4, :], ACT.Copy))
                        a.mark(name, l, k)
                    elif name == "sample_pv" and k == 3:
                        wait_step(l, name, k)
                        give(act.activation(o_ab[:, :, SEQ:TOK], side[:, 2, :].rearrange("p (c n) -> p c n", c=8),
                                            ACT.Copy))
                        marks[(name, l, k)] = (act_given, given[0])
                for g in gated_at(beat, 1):
                    gate_high(l, g)
                for name, k, _ in STEPS.get(beat - 1, ()):
                    if name in ("k_norm", "q_norm"):
                        vec("normed", l, (name, k))
                        for q in range(4):
                            ins = act.activation(tc[32 * q:32 * q + 32, :, :], ta[32 * (q ^ 1):32 * (q ^ 1) + 32, :, :],
                                                 ACT.Copy)
                            if q == 3:
                                ins.then_inc(swapped, 1)
                            else:
                                a(ins)
                if TAKEN_AT.get(beat, 0) >= G_CZ:
                    gate_take(l, TAKEN_AT[beat])
                if beat in STACK_AT:
                    n = STACK_AT.index(beat)
                    half = n % 2
                    rows = slice(32 * half, 32 * half + 32)
                    if n < 2:
                        a(act.activation(k_stack[0:32, half, :], ko_tok[rows, 2, :], ACT.Copy))
                        last = act.activation(k_stack[32:64, half, :], ko_tok[rows, 2, :], ACT.Copy)
                    else:
                        a(act.activation(v_stack[half][rows, :], v_gla[rows, 2, :], ACT.Copy))
                        last = act.activation(v_stack[half][64:96, :], v_gla[rows, 2, :], ACT.Copy)
                    last.then_inc(stack_hi, 1)
                for k in range(1, 8):
                    if beat == 17 + 2 * k:
                        B = LEVELS[k - 1]
                        e4, n = segs(lev_e, B)
                        vec("level_gap", l, k)
                        a(act.activation(e4[:, :, :, 0:B], e4[:, :, :, 0:B], ACT.Exp, scale=-1.0))
                        act.activation(e4[:, :, :, B:2 * B], e4[:, :, :, B:2 * B], ACT.Exp).then_inc(level_exp, 1)
                if beat == 34:
                    vec("level", l, 7)
                    act.wait_ge(level_k, 7 * l + 7)
                    a(act.activation(edge[:, :, 0:2], cb[:, :, 0:SEQ].rearrange("p h (a b) -> p h a b", b=P)[:, :, :, P - 1],
                                     ACT.Exp))
                    a(act.activation(edge[:, :, 2:], cb[:, :, SEQ:TOK].rearrange("p h (a b) -> p h a b", b=TS)[:, :, :, TS - 1],
                                     ACT.Exp))
                    give(act.activation(lev_e[:, :, :], cb[:, :, :], ACT.Exp))
                for k in range(2):
                    if beat == 68 + 2 * k:
                        if k:
                            wait_step(l, "gla_norm", 0)
                        give(act.activation(squares[:, :, :], o_c[:, 4 * k:4 * k + 4, :], ACT.Square))
                for name, k, at in [("k_norm", 0, 70)] + [("q_norm", k, 77 + 4 * k) for k in range(4)]:
                    if beat == at:
                        s, n = marks[("taken", l, G_K if name == "k_norm" else G_Q + k)]
                        act.wait_ge(s, n)
                        if name == "q_norm":
                            vec("roped", l, ("q_norm", k - 1) if k else ("k_norm", 0))
                        a(act.activation(tc[:, :, :], ta[:, :, :], ACT.Square))
                        a.mark("head_squares", l, (name, k))
            def mix_body(l, i):
                Q0 = BEATS * l + IN_BEATS
                G0 = GROUPS * l + 1 + N_IN
                b = 0
                for jj in range(2):
                    for n in range(3):
                        for part in range(6):
                            split_hi(i * 36 + (Q0 + b + 2), Q0 + b + 2)
                            b += 1
                            if part == 3:
                                act.wait_ge(main_free, i * 12 + (G0 + 6 * jj + 2 * n + 1))
                                act.activation(tb[:, :, :], ta[:, :, :], ACT.Sigmoid).then_inc(act_given, 1)

            for l in range(DEPTH):
                last_layer = l == DEPTH - 1
                for beat in range(IN_BEATS):
                    Q = BEATS * l + beat
                    if l == 0 and beat == 0:
                        first_x(0)
                        first_x(1)
                        split_hi(0, 0)
                        first_x(2)
                        first_x(3)
                        split_hi(1, 1)
                    split_hi(Q + 2, Q + 2)
                    scalar_part(l, beat)
                with act.Fori(0, 4) as i:
                    mix_body(l, i)
                table[0] = None
                given[0] += 24
                Q0 = BEATS * l + IN_BEATS + MIX_BEATS
                with act.Fori(0, 3 if last_layer else 4) as i:
                    for b in range(8):
                        split_hi(i * 8 + (Q0 + b + 2), Q0 + b + 2)
                if last_layer:
                    for b in range(6):
                        split_hi(24 + Q0 + b + 2, 24 + Q0 + b + 2)

        @block.sync
        def _(sp):
            def load(Q, s0):
                if s0 >= 4:
                    sp.wait_ge(lo_ready, Q * 2 - 6)
                sp.dma_start(raw[s0 % 4][:, :], ins["w_stream"][bass.ds(Q, 1)].rearrange("a p n -> (a p) n")
                             if not isinstance(Q, int) else ins["w_stream"][Q]).then_inc(raw_in[s0 % 4], 16)

            for Q in range(4):
                load(Q, Q)
            total = BEATS * DEPTH
            with sp.Fori(1, total // 4) as i:
                for s in range(4):
                    load(i * 4 + s, 4 + s)
            for Q in range(total // 4 * 4, total):
                load(Q, Q)

        @block.gpsimd
        def _(pool):
            def load(dst, src, s):
                pool.dma_start(dst, src).then_inc(s, 16)

            def store_y(l, j):
                pool.wait_ge(main_free, GROUPS * l + 1 + N_IN + 6 * PAIRS + j + 1)
                load((outs["y"] if l == DEPTH - 1 else ins["y_mid"])[j], (ta, tb)[j % 2][:, :, :], y_out[j % 2])

            load(const[:, :], ins["consts"], consts_in)
            load(amask_p[:, :], ins["amask_p"], consts_in)
            load(amask_s[:, :], ins["amask_s"], consts_in)
            load(gmask_f[:, :, :], ins["gmask"], consts_in)
            for l in range(DEPTH):
                if l:
                    pool.wait_ge(half_used, last_half(l - 1, IN_BEATS + MIX_BEATS - 1))
                load(w_gate[0:RANK, :], ins["w_gate"][l], w_gate_in)
                load(w_pool[:, :, :], ins["w_pool"][l], w_pool_in)
                if l:
                    pool.wait_ge(half_used, last_half(l - 1, BEATS - 1))
                else:
                    wait_mark(pool, "masks", 0, 0)
                load(hist[:, :, :], ins["hist"][l], hist_in)
                load(outs["k_window"][l], ins["cache_k_tok"][l, :, TS:WINDOW, :], window_out)
                load(outs["new_v_s"][l, :, 0:WINDOW - TS, :], ins["cache_v_tok"][l, :, TS:WINDOW, :], window_out)
                for k in range(1, 8):
                    B = LEVELS[k - 1]
                    w = segs(lev_e, B)[1] * 2 * B
                    s, n = marks[("taken", l, G_CV - 1)]
                    if k == 1:
                        pool.wait_ge(s, n)
                        wait_mark(pool, "keys_clear", l, 0)
                    else:
                        pool.wait_ge(step_done, N_STEPS * l + STEP_NO[("level", k - 1)] + 1)
                    pool.wait_ge(level_exp, 7 * l + k)
                    kk, kc, ke = (even_blocks(z, B, w) for z in (lev_k, ck, lev_e))
                    pool.tensor_tensor(kk, kc, ke, ALU.mult).then_inc(level_k, 1)
                wait_mark(pool, "carry", l, 0)
                for k in range(STATES):
                    load(state[:, k, :, :], ins["state"][l, k], state_in[k])
                s, n = marks[("hist", l, 3)]
                pool.wait_ge(s, n)
                load(outs["hist"][l], hist[:, :, :], hist_out)
                wait_mark(pool, "second_state", l, 0)
                load(outs["state_p"][l], s1[:, :, :], s2_out)
                for k in range(8):
                    wait_mark(pool, "sample_state", l, k)
                    load(outs["state_s"][l, k], state[:, k % STATES, :, :], state_out[k % STATES])
                    if 1 <= k and k - 1 + STATES < 8:
                        m = k - 1
                        pool.wait_ge(state_out[m % STATES], 16 * state_load(l, m))
                        load(state[:, m % STATES, :, :], ins["state"][l, m + STATES], state_in[m % STATES])
                for m in range(8 - STATES, 8):
                    pool.wait_ge(state_out[m % STATES], 16 * state_load(l, m))
                load(cache_k[:, :, :, :], ins["cache_k"][l], caches_in)
                load(cache_v[:, :, :], ins["cache_v"][l], caches_in)
                wait_mark(pool, "roped", l, ("k_norm", 0))
                load(outs["k_new"][l], k_a[:, :, P:TOK], kv_out)
                s, n = marks[("taken", l, G_V)]
                pool.wait_ge(s, n)
                load(outs["v_new"][l], tb[:, :, P:SEQ], kv_out)
                wait_mark(pool, "kv_turn", l, 0)
                load(outs["new_v_s"][l, :, WINDOW - TS:WINDOW, :], v_tok[0:SMP, 2, :], kv_out)
                for j in range(8):
                    slot = (ta, tb)[j % 2]
                    if j < 2:
                        wait_mark(pool, "merged", l, 0)
                    else:
                        pool.wait_ge(y_out[j % 2], 16 * (4 * l + (j - 2) // 2 + 1))
                        if l < DEPTH - 1:
                            wait_mark(pool, "xg", l + 1, j - 2)
                    load(slot[:, :, :], ins["x_pairs"][j] if l == 0 else ins["y_mid"][j], res_in[j % 2])
                    if j >= 1:
                        store_y(l, j - 1)
                store_y(l, 7)
                for i in range(2):
                    pool.wait_ge(y_out[i], 64 * (l + 1))
            pool.wait_ge(hist_out, 16 * DEPTH)
            pool.wait_ge(s2_out, 16 * DEPTH)
            pool.wait_ge(kv_out, 48 * DEPTH)
            pool.wait_ge(window_out, 32 * DEPTH)

        @block.tensor
        def _(pe):
            def free_banks(l, step):
                i = STEP_NO[step]
                for b in BANKS[step]:
                    for m in range(i - 1, i - 1 - N_STEPS, -1):
                        s = ORDER[m % N_STEPS]
                        if b in BANKS[s]:
                            ll = l + (m // N_STEPS)
                            if ll >= 0 and s in READ_BY:
                                for key in READ_BY[s]:
                                    wait_mark(pe, key[0], ll, key[1])
                            break

            READ_BY = {("gate", 0): [("gate_in", 0)], ("k_turn", 0): [("k_turn", 0)],
                       ("first_chunk", 0): [("first_chunk", 0)],
                       ("second_chunk", 0): [("second_chunk", 0), ("second_state", 0)],
                       ("kv_turn", 0): [("kv_turn", 0)], ("k_norm", 0): [("head_ms", ("k_norm", 0))]}
            for k in range(8):
                READ_BY[("level", k)] = [("att", k)]
                READ_BY[("sample_gla", k)] = [("sample_state", k)]
                READ_BY[("scores", k)] = [("masked", k)]
                READ_BY[("p_turn", k)] = [("p_turn", k)]
                READ_BY[("pv", k)] = [("pv", k)]
            READ_BY[("sample_gla", 7)].append(("sample_gla", 7))
            for k in range(4):
                READ_BY[("v_turn_prompt", k)] = [("v_turn_prompt", k)]
                READ_BY[("v_turn_sample", k)] = [("v_turn_sample", k)]
                READ_BY[("pool", k)] = [("pooled", k)]
                READ_BY[("q_norm", k)] = [("head_ms", ("q_norm", k))]
                READ_BY[("sample_scores", k)] = [("sample_masked", k)]
                READ_BY[("sample_p_turn", k)] = [("sample_p_turn", k)]
            READ_BY[("sample_pv", 3)] = [("sample_pv", 3)]
            for k in range(2):
                READ_BY[("gla_norm", k)] = [("gla_ms", k)]

            def mm(out, lhsT, rhs, start=True, stop=True):
                return pe.matmul(out, lhsT, rhs, start=start, stop=stop)

            def turn(out, src):
                return pe.transpose(out, src, ident[0:src.shape[0], 0:src.shape[0]])

            def block_products(Q, s0, G, tiles, hi, lo, k0, first, last, narrow=False):
                base = 2 * (G % 2)
                for s in range(2):
                    i = (2 * s0 + s) % 4
                    pe.wait_ge(lo_ready, Q * 2 + (s + 1))
                    nk = 4 if narrow else 2
                    w = 128 if narrow else 256
                    for kk in range(nk):
                        k = k0 + nk * s + kk
                        for t in range(tiles):
                            c = kk * w + t * P
                            out = main[:, base + t, 0:TOK]
                            st = first and s == 0 and kk == 0
                            sp_ = last and s == 1 and kk == nk - 1
                            mm(out, w_hi[i][:, c:c + P], hi[:, k, :], st, False)
                            mm(out, w_hi[i][:, c:c + P], lo[:, k, :], False, False)
                            ins_ = mm(out, w_lo[i][:, c:c + P], hi[:, k, :], False, sp_)
                    ins_.then_inc(half_used, 1)

            def side_step(l, name, k, banks):
                free_banks(l, (name, k))
                wm = lambda *key: wait_mark(pe, *key)
                if name == "gate":
                    wm("lr", l, 0)
                    wm("rms_taken", l, 0)
                    pe.wait_ge(w_gate_in, 16 * l + 16)
                    for h in range(GH):
                        last = mm(side[:, h, 0:TOK], w_gate[0:RANK, DK * h:DK * h + DK], ta[0:RANK, 0, :])
                elif name == "level":
                    if k == 0:
                        wm("taken", l, G_CV - 1)
                        wm("decay", l, 0)
                        kk, qq = ck, cq
                    else:
                        wm("level", l, k)
                        pe.wait_ge(level_k, 7 * l + k)
                        kk, qq = lev_k, lev_q
                    for c in range(3 if k <= 3 else 2):
                        lo, n = (P * c, P) if c < 2 else (SEQ, SMP)
                        for h in range(GH):
                            q, m = qq[:, h:h + 1, lo:lo + n], n
                            if k:
                                q, m = odd_blocks(qq[:, h:h + 1, :], LEVELS[k - 1], lo, lo + n), n // 2
                                q = q.rearrange("p h a b -> p (h a) b")
                            else:
                                q = q.rearrange("p h t -> p (h t)")
                            last = mm(side[0:n, c, m * h:m * h + m], kk[:, h, lo:lo + n], q)
                elif name == "v_turn_prompt":
                    wm("taken", l, G_CV + k)
                    for c in range(2):
                        for t in range(2):
                            last = turn(side[:, 3, 256 * c + P * t:256 * c + P * t + P],
                                        o_c[:, 2 * k + t, P * c:P * c + P])
                elif name == "v_turn_sample":
                    for t in range(2):
                        last = turn(side[0:SMP, 3, P * t:P * t + P], o_c[:, 2 * k + t, SEQ:TOK])
                elif name == "k_turn":
                    wm("carry", l, 0)
                    for h in range(GH):
                        for c in range(2):
                            turn(side[:, c, DK * h:DK * h + DK], lev_k[:, h, P * c:P * c + P])
                        last = turn(side[0:SMP, 2, DK * h:DK * h + DK], lev_k[:, h, SEQ:TOK])
                elif name == "pool":
                    wm("diff", l, k)
                    pe.wait_ge(w_pool_in, 16 * l + 16)
                    for t in range(2):
                        for c in range(2):
                            last = mm(side[:, 2 + t, 0:TOK], w_pool[:, 2 * k + c, P * t:P * t + P], diff[:, c, :],
                                      c == 0, c == 1)
                elif name == "first_chunk":
                    wm("k_turn", l, 0)
                    wm("v_turn_sample", l, 3)
                    wm("att", l, 7)
                    for h in range(GH):
                        mm(side[:, h // 2, 256 * (h % 2):256 * (h % 2) + 256], ko_tok[:, 0, DK * h:DK * h + DK],
                           v_gla[:, 0, DV * h:DV * h + DV])
                    for c in range(8):
                        last = mm(side[:, 2 + c // 4, P * (c % 4):P * (c % 4) + P], v_gla[:, 0, P * c:P * c + P],
                                  att_p[:, 0, P * (c // 2):P * (c // 2) + P])
                elif name == "second_chunk":
                    wm("first_chunk", l, 0)
                    for c in range(8):
                        h, out = c // 2, side[:, c // 4, P * (c % 4):P * (c % 4) + P]
                        mm(out, v_gla[:, 1, P * c:P * c + P], att_p[:, 1, P * h:P * h + P], True, False)
                        mm(out, s1[:, h, P * (c % 2):P * (c % 2) + P], lev_q[:, h, P:SEQ], False, True)
                    for h in range(GH):
                        last = mm(side[:, 2 + h // 2, 256 * (h % 2):256 * (h % 2) + 256],
                                  ko_tok[:, 1, DK * h:DK * h + DK], v_gla[:, 1, DV * h:DV * h + DV])
                elif name == "sample_gla":
                    h, half = divmod(k, 2)
                    pe.wait_ge(state_in[k % STATES], 16 * state_load(l, k))
                    wm("k_sel", l, k)
                    for t in range(2):
                        c = 2 * h + t
                        n = 32 * half
                        mm(side[:, 3, SMP * c + n:SMP * c + n + 32], v_gla[0:SMP, 2, P * c:P * c + P],
                           att_s[0:SMP, SMP * h + n:SMP * h + n + 32], True, False)
                        for b in range(4):
                            n = 32 * half + TS * b
                            mm(side[:, 3, SMP * c + n:SMP * c + n + TS], state[:, k % STATES, b, P * t:P * t + P],
                               lev_q[:, h, SEQ + n:SEQ + n + TS], False, b == 3)
                    for b in range(4):
                        last = mm(side[:, b // 2, 256 * (b % 2):256 * (b % 2) + 256], k_sel[0:96, b, :],
                                  v_stack[half][0:96, DV * h:DV * h + DV])
                elif name == "gla_norm":
                    wm("squares", l, k)
                    for i in range(2):
                        last = mm(side[:, i, 0:TOK], ones[:, :], squares[:, 2 * i, :])
                elif name in ("k_norm", "q_norm"):
                    wm("head_squares", l, (name, k))
                    for t in range(2):
                        last = mm(side[:, 2 + t, 0:TOK], head_ones, tc[:, t, :])
                elif name == "kv_turn":
                    wm("taken", l, G_V)
                    for t in range(2):
                        for c in range(2):
                            turn(side[:, 2, 256 * c + P * t:256 * c + P * t + P], tb[:, t, P * c:P * c + P])
                        last = turn(side[0:SMP, 3, P * t:P * t + P], tb[:, t, SEQ:TOK])
                elif name == "scores":
                    wm("roped", l, ("q_norm", k // 2))
                    kt = k // 4
                    for i in range(2):
                        rows = slice(HD * i, HD * i + HD)
                        mm(side[:, banks[i], 0:256], q_a[rows, k, P:SEQ], k_a[rows, kt, 0:SEQ])
                        last = mm(side[:, banks[i], 256:384], q_a[rows, k, 0:P], k_a[rows, kt, 0:P])
                elif name == "p_turn":
                    wm("probs", l, k)
                    for i in range(2):
                        for c in range(3):
                            last = turn(side[:, banks[i], P * c:P * c + P],
                                        probs[k % 2][:, 384 * i + P * c:384 * i + P * c + P])
                elif name == "pv":
                    wm("p_turn", l, k)
                    wm("kv_turn", l, 0)
                    p = probs[k % 2]
                    for i in range(2):
                        kv = 2 * (k // 4) + i
                        rows = slice(HD * i, HD * i + HD)
                        vc = slice(HD * kv, HD * kv + HD)
                        n = 384 * i
                        early, late = side[rows, banks[0], 384:512], side[rows, banks[1], 384:512]
                        mm(late, v_tok[:, 0, vc], p[:, n:n + P], True, False)
                        mm(late, v_tok[:, 1, vc], p[:, n + P:n + 2 * P], False, True)
                        last = mm(early, v_tok[:, 0, vc], p[:, n + 2 * P:n + 3 * P])
                elif name == "sample_scores":
                    pe.wait_ge(caches_in, 32 * l + 32)
                    for b in range(2):
                        for i in range(2):
                            qs = q_s[:, i, 2 * k + b, :, :, :].rearrange("p j g t -> p (j g t)")
                            out = side[64 * i:64 * i + 64, banks[0], 192 * b:192 * b + 192]
                            mm(out[:, 0:WINDOW], qs, cache_k[:, i, 2 * k + b, :])
                            last = mm(out[:, WINDOW:], qs, k_a[:, i, SEQ:TOK])
                elif name == "sample_p_turn":
                    wm("sample_probs", l, k)
                    p = probs[k % 2]
                    for b in range(2):
                        turn(side[:, banks[0], P * b:P * b + P], p[:, 192 * b:192 * b + WINDOW])
                        last = turn(side[0:SMP, banks[0], 256 + P * b:384 + P * b], p[:, 192 * b + WINDOW:192 * b + 192])
                elif name == "sample_pv":
                    wm("sample_p_turn", l, k)
                    p = probs[k % 2]
                    for b in range(2):
                        for kv in range(KVH):
                            rows = slice(HD * (kv % 2), HD * (kv % 2) + HD)
                            vc = slice(HD * kv, HD * kv + HD)
                            o4 = side[rows, 2, :].rearrange("p (j t) -> p j t", j=8)
                            n = TS * (2 * k + b)
                            out = o4[:, 4 * (kv // 2):4 * (kv // 2) + 4, n:n + TS]
                            mm(out, cache_v[:, 2 * k + b, vc], p[:, P * b + 32 * kv:P * b + 32 * kv + 32], True, False)
                            last = mm(out, v_tok[0:SMP, 2, vc], p[0:SMP, 256 + P * b + 32 * kv:256 + P * b + 32 * kv + 32],
                                      False, True)
                last.then_inc(step_done, 1)

            def wait_main(G0, value):
                if G0 >= 2:
                    pe.wait_ge(main_free, value)

            for l in range(DEPTH):
                for beat in range(IN_BEATS):
                    Q = BEATS * l + beat
                    if LR_AT <= beat < LR_AT + LR_BEATS:
                        G, part = GROUPS * l + LR_GROUP, beat - LR_AT
                        if part == 0:
                            wait_main(G, G - 1)
                        block_products(Q, Q, G, 1, xg_hi, xg_lo, 8 * part, part == 0, part == 1, narrow=True)
                    else:
                        g, part = divmod(beat if beat < LR_AT else beat - LR_BEATS, 4)
                        G = GROUPS * l + group_no(g)
                        if part == 0:
                            wait_main(G, G - 1)
                        if g == 0:
                            for j in (2 * part, 2 * part + 1):
                                wait_mark(pe, "xg", l, j)
                        block_products(Q, Q, G, 2, xg_hi, xg_lo, 4 * part, part == 0, part == 3)
                    if beat == 3:
                        wait_mark(pe, "sq_sum", l, 0)
                        if l:
                            free_banks(l, ORDER[0])
                        mm(rms_psum, ones[:, :], sq_sum[:, :]).then_inc(rms_done, 1)
                    for name, k, banks in STEPS.get(beat, ()):
                        side_step(l, name, k, banks)
                wait_mark(pe, "branch", l, G_AZ - 1)
                Q0 = BEATS * l + IN_BEATS
                G0 = GROUPS * l + 1 + N_IN
                with pe.Fori(0, PAIRS // 2) as i:
                    b = 0
                    G = G0
                    for jj in range(2):
                        for n in MIX_ORDER:
                            pe.wait_ge(main_free, i * 12 + (G - 1))
                            for part in range(4):
                                block_products(i * 36 + (Q0 + b), Q0 + b, G, 2, xg_hi, xg_lo, 4 * part,
                                               part == 0, part == 3)
                                b += 1
                            G += 1
                            pe.wait_ge(main_free, i * 12 + (G - 1))
                            if n == BR_A:
                                wait_mark(pe, "branches", l, 0)
                            for part in range(2):
                                block_products(i * 36 + (Q0 + b), Q0 + b, G, 2, br_hi[n], br_lo[n], 4 * part,
                                               part == 0, part == 1)
                                b += 1
                            G += 1
                Q0 += MIX_BEATS
                G0 += 6 * PAIRS
                wait_mark(pe, "merged_first", l, 0)
                with pe.Fori(0, PAIRS // 2) as i:
                    for jj in range(2):
                        pe.wait_ge(main_free, i * 2 + (G0 + jj - 1))
                        for part in range(4):
                            b = 4 * jj + part
                            if part == 3:
                                wait_mark(pe, "merged", l, 0)
                            block_products(i * 8 + (Q0 + b), Q0 + b, G0 + jj, 2, mg_hi, mg_lo, 4 * part,
                                           part == 0, part == 3)


def _constants():
    import numpy as np
    p = np.arange(P)
    c = np.zeros((P, C_END), np.float32)
    pos = np.concatenate([np.arange(SEQ), np.tile(PAST + np.arange(TS), NB)]).astype(np.float32)
    inv = np.power(10000.0, -np.arange(HD // 2) * (2.0 / HD)).astype(np.float32)
    ang = (pos[None, :] * inv[p % (HD // 2)][:, None]).astype(np.float32)
    sign = np.where(p % HD < HD // 2, -1.0, 1.0)[:, None]
    c[:, C_COS:C_COS + TOK] = np.cos(ang.astype(np.float64))
    c[:, C_SIN:C_SIN + TOK] = sign * np.sin(ang.astype(np.float64))
    c[:, C_IDENT:C_IDENT + P] = np.eye(P)
    c[:, C_BLOCK:C_BLOCK + P] = p[:, None] // HD == p[None, :] // HD
    t = np.arange(TOK)
    c[:, C_KEEP:C_KEEP + TOK] = np.where(t < SEQ, t % P != 0, t % TS != 0)
    for g in range(4):
        c[:, C_INVC + 16 * g:C_INVC + 16 * g + 16] = 1.0 / np.minimum(2 << g, np.arange(16) + 1)
    c[:, C_BSEL:C_BSEL + 4] = p[:, None] % 32 // TS == np.arange(4)[None, :]
    far = np.float32(-1e30)
    i, j = p[:, None], p[None, :]
    am = np.concatenate([np.where(j >= i, 0, far), np.where(j <= i, 0, far)], axis=1)
    t = p[:, None] % TS
    s = np.arange(SMP)[None, :]
    new = [np.where((s // TS == b) & (s % TS <= t), 0, far) for b in range(NB)]
    asm = np.concatenate([np.where(j >= t, 0, far)] + new, axis=1)
    gm = np.zeros((P, 8, P), np.float32)
    gm[:, 0] = i == j
    for k, B in enumerate(LEVELS):
        gm[:, k + 1] = (i // (2 * B) == j // (2 * B)) & (i % (2 * B) < B) & (j % (2 * B) >= B)
    return c, am, asm, gm


def kernel(**inputs):
    import ml_dtypes
    import numpy as np
    import concourse.bacc as bacc
    from concourse.bass_utils import run_bass_kernel_spmd

    x = {n: np.asarray(a) for n, a in inputs.items()}
    pair_heads = [h for j in range(8) for h in (8 * (j // 4) + j % 4, 8 * (j // 4) + j % 4 + 4)]
    head_rows = np.concatenate([np.arange(HD * h, HD * h + HD) for h in pair_heads])
    cols = {"a_q": head_rows, "a_k": 1024 + np.arange(256), "a_v": 1280 + np.arange(256), "a_z": 1536 + head_rows,
            "b_u": 2560 + np.arange(1024), "b_z": 3584 + np.arange(1024), "c_q": 4608 + np.arange(512),
            "c_k": 5120 + np.arange(512), "c_v": 5632 + np.arange(1024), "c_z": 6672 + np.arange(1024)}
    order = np.concatenate([cols[n] for n in ("c_q", "c_k", "c_v", "b_u", "b_z", "a_k", "a_v", "a_q", "c_z", "a_z")])
    lr0, gate0 = 6656, 7696
    w = np.zeros((DEPTH, BEATS, P, 1024), np.float32)
    for l in range(DEPTH):
        win, wbr, wout = x["w_in"][l], x["w_branch"][l], x["w_out"][l]
        lr = w[l, LR_AT:LR_AT + LR_BEATS].reshape(2, P, 8, 128)
        lr[:, :, :, 0:RANK] = win[:, lr0:lr0 + RANK].reshape(2, 8, P, RANK).transpose(0, 2, 1, 3)
        m = win[:, order].reshape(4, 4, P, N_IN, 256)
        m = m.transpose(3, 0, 2, 1, 4).reshape(4 * N_IN, P, 1024)
        w[l, 0:LR_AT] = m[:LR_AT]
        w[l, LR_AT + LR_BEATS:IN_BEATS] = m[LR_AT:]
        mix = w[l, IN_BEATS:IN_BEATS + MIX_BEATS].reshape(PAIRS, 3, 6, P, 4, 256)
        gates = win[:, gate0:].reshape(4, 4, P, 3, PAIRS, 256)
        for i, n in enumerate(MIX_ORDER):
            mix[:, i, 0:4] = gates[:, :, :, n].transpose(3, 0, 2, 1, 4)
            rows = wbr[n][head_rows] if n == BR_A else wbr[n]
            mix[:, i, 4:6] = rows.reshape(2, 4, P, PAIRS, 256).transpose(3, 0, 2, 1, 4)
        w[l, IN_BEATS + MIX_BEATS:] = wout.reshape(4, 4, P, PAIRS, 256).transpose(3, 0, 2, 1, 4).reshape(32, P, 1024)

    def cm(a, n):
        return a.reshape(a.shape[:-1] + (n, P)).swapaxes(-1, -2)

    tok = np.concatenate([x["x_prompt"][0], x["x_sample"].reshape(SMP, D)], axis=0)
    par = np.zeros((P, DEPTH, R_END), np.float32)
    for l in range(DEPTH):
        par[:, l, R_NG:R_NG + 16] = cm(x["norm_g"][l], 16)
        par[:, l, R_QG] = np.tile(x["q_norm_g"][l], 2)
        par[:, l, R_KG] = np.tile(x["k_norm_g"][l], 2)
        par[:, l, R_SINK:R_SINK + 16] = x["sinks"][l][pair_heads][None, :]
        par[:, l, R_SSINK] = np.repeat(x["sinks"][l], TS)
        par[:, l, R_PS:R_PS + 8] = cm(x["pool_scale"][l], 8)
        par[:, l, R_BG:R_BG + 4] = cm(x["b_gate"][l], 4)
        par[:, l, R_GG:R_GG + 2] = cm(x["gla_norm_g"][l], 2)
    hist = np.zeros((DEPTH, P, 8, 1 + NB, HIST), np.float32)
    hist[:, :, :, 1:] = x["state_pool"].reshape(DEPTH, NB, HIST, 8, P).transpose(0, 4, 3, 1, 2)
    consts, amask_p, amask_s, gmask = _constants()
    ck = x["cache_a_k"].reshape(DEPTH, NB, WINDOW, 2, P)
    feeds = {
        "w_stream": w.reshape(DEPTH * BEATS, P, 1024),
        "x_pairs": tok.T.reshape(PAIRS, 2, P, TOK).transpose(0, 2, 1, 3),
        "consts": consts,
        "amask_p": amask_p.astype(ml_dtypes.bfloat16),
        "amask_s": amask_s.astype(ml_dtypes.bfloat16),
        "gmask": gmask,
        "params": par,
        "hist": hist.reshape(DEPTH, P, 8, (1 + NB) * HIST),
        "w_pool": x["w_pool"].reshape(DEPTH, 4, 2, P, 256).transpose(0, 3, 1, 2, 4).reshape(DEPTH, P, 8, 256),
        "w_gate": x["w_gate_lr"],
        "state": x["state_gla"].reshape(DEPTH, 2, 4, GH, DK, DV).transpose(0, 3, 1, 4, 2, 5).reshape(DEPTH, 8, DK, 4, DV),
        "cache_k": ck.transpose(0, 4, 3, 1, 2),
        "cache_v": x["cache_a_v"].reshape(DEPTH, NB, WINDOW, 256).transpose(0, 2, 1, 3),
        "cache_k_tok": x["cache_a_k"].reshape(DEPTH, NB, WINDOW, 256),
        "cache_v_tok": x["cache_a_v"].reshape(DEPTH, NB, WINDOW, 256),
    }
    shapes = {"y": (PAIRS, P, 2, TOK), "k_new": (DEPTH, P, 2, P + SMP), "v_new": (DEPTH, P, 2, P),
              "k_window": (DEPTH, NB, WINDOW - TS, 256), "new_v_s": (DEPTH, NB, WINDOW, 256),
              "hist": (DEPTH, P, 8, (1 + NB) * HIST), "state_p": (DEPTH, DK, GH, DV), "state_s": (DEPTH, 8, DK, 4, DV)}
    nc = bacc.Bacc("TRN2", target_bir_lowering=False, num_devices=1)
    arrays = {f"in_{n}": np.ascontiguousarray(a) for n, a in feeds.items()}
    ins = {n: nc.dram_tensor(f"in_{n}", a.shape, mybir.dt.from_np(a.dtype), kind="ExternalInput").ap()
           for n, a in feeds.items()}
    ins["y_mid"] = nc.dram_tensor("y_mid", (PAIRS, P, 2, TOK), F32, kind="Internal").ap()
    outs = {n: nc.dram_tensor(f"out_{n}", s, F32, kind="ExternalOutput").ap() for n, s in shapes.items()}
    trunk(nc, ins, outs)
    r = run_bass_kernel_spmd(nc, [arrays], core_ids=[0]).results[0]
    o = {n: np.asarray(r[f"out_{n}"]).reshape(s) for n, s in shapes.items()}

    y = o["y"].transpose(0, 2, 1, 3).reshape(D, TOK).T
    kn = o["k_new"].transpose(0, 3, 2, 1).reshape(DEPTH, P + SMP, KVH, HD)
    vn = o["v_new"].transpose(0, 3, 2, 1).reshape(DEPTH, 1, P, KVH, HD)
    kw = np.concatenate([o["k_window"].reshape(DEPTH, NB, WINDOW - TS, KVH, HD),
                         kn[:, P:].reshape(DEPTH, NB, TS, KVH, HD)], axis=2)
    hs = o["hist"].reshape(DEPTH, P, 8, 1 + NB, HIST).transpose(0, 3, 4, 2, 1).reshape(DEPTH, 1 + NB, HIST, BRANCH)
    ss = o["state_s"].reshape(DEPTH, GH, 2, DK, 4, DV).transpose(0, 2, 4, 1, 3, 5).reshape(DEPTH, NB, GH, DK, DV)
    return (y[None, :SEQ], y[SEQ:].reshape(NB, TS, D),
            kn[:, None, :P], vn, hs[:, 0:1], o["state_p"].transpose(0, 2, 1, 3)[:, None],
            kw, o["new_v_s"].reshape(DEPTH, NB, WINDOW, KVH, HD), hs[:, 1:], ss)
```
